# Optimizing a Trainium2 kernel written in Bass

```python
import math
import jax, jax.numpy as jnp
from jax import lax
import numpy as np

D_MODEL = 1024
BATCH = 1
SEQ = 512
DEPTH = 2

PLE_DIM = 256
A_HEADS = 8
A_HEAD_DIM = 64
IDX_HEADS = 4
IDX_DIM = 64
TOPK_MAX = 256
B_HEADS = 8
B_NOPE = 64
B_ROPE = 32
B_V = 64
Q_LORA = 384
KV_LORA = 256
C_CH = 512
CONV_W = 31
N_BRANCH = 3
BRANCH_W = 512
FF = (8 * D_MODEL + 3 * 256 - 1) // (3 * 256) * 256

ROPE_THETA = 10000.0
Q_BLOCK = 128
LN_EPS = 1e-5
RMS_EPS = 1e-6
ALPHA = (2 * DEPTH) ** 0.25
OUT_SCALE = (8 * DEPTH) ** -0.25

IN_SIZES = (A_HEADS * A_HEAD_DIM, A_HEAD_DIM, A_HEAD_DIM,
            IDX_HEADS * IDX_DIM, IDX_DIM, IDX_HEADS,
            Q_LORA, KV_LORA, B_ROPE,
            2 * C_CH,
            N_BRANCH * D_MODEL)
IN_SPLITS = tuple(int(v) for v in np.cumsum(IN_SIZES)[:-1])
N_IN = int(sum(IN_SIZES))

kernel_name = "hybrid_dsa_mla_conformer_deepnorm"

def layer_norm(x, g, b):
    xf = x.astype(jnp.float32)
    mu = xf.mean(-1, keepdims=True)
    var = jnp.square(xf - mu).mean(-1, keepdims=True)
    return ((xf - mu) * lax.rsqrt(var + LN_EPS) * g + b).astype(x.dtype)

def rms_norm(x, g):
    xf = x.astype(jnp.float32)
    return (xf * lax.rsqrt(jnp.mean(xf * xf, -1, keepdims=True) + RMS_EPS) * g).astype(x.dtype)

def rope_tables(positions, dim):
    inv = 1.0 / (ROPE_THETA ** (jnp.arange(0, dim, 2, dtype=jnp.float32) / dim))
    ang = positions.astype(jnp.float32)[..., None] * inv
    return jnp.cos(ang), jnp.sin(ang)

def apply_rope(x, cos, sin):
    shp = cos.shape[:2] + (1,) * (x.ndim - 3) + cos.shape[-1:]
    c, s = cos.reshape(shp), sin.reshape(shp)
    x1, x2 = jnp.split(x.astype(jnp.float32), 2, axis=-1)
    return jnp.concatenate([x1 * c - x2 * s, x2 * c + x1 * s], axis=-1).astype(x.dtype)

def to_blocks(a, nb):
    return a.reshape((a.shape[0], nb, Q_BLOCK) + a.shape[2:]).swapaxes(0, 1)

def from_blocks(a):
    a = a.swapaxes(0, 1)
    return a.reshape((a.shape[0], a.shape[1] * a.shape[2]) + a.shape[3:])

def dsa_attention(q, k, v, q_idx, k_idx, w_idx):
    B, S, H, D = q.shape
    nb = S // Q_BLOCK
    top_k = min(TOPK_MAX, S // 4)
    scale = D ** -0.5
    kpos = jnp.arange(S)
    gather = jax.vmap(lambda t, i: t[i])

    def one_block(args):
        qb, qib, wb, i = args
        qpos = i * Q_BLOCK + jnp.arange(Q_BLOCK)
        logits = jnp.einsum('bqhd,bkd->bqhk', qib, k_idx, preferred_element_type=jnp.float32) * (IDX_DIM ** -0.5)
        score = jnp.einsum('bqh,bqhk->bqk', wb.astype(jnp.float32) * (IDX_HEADS ** -0.5), jax.nn.relu(logits))
        causal = kpos[None, :] <= qpos[:, None]
        score = jnp.where(causal[None], score, -jnp.inf)
        _, sel = lax.top_k(score, top_k)
        valid = sel <= qpos[None, :, None]
        k_sel = gather(k, sel)
        v_sel = gather(v, sel)
        s = jnp.einsum('bqhd,bqkd->bqhk', qb, k_sel, preferred_element_type=jnp.float32) * scale
        s = jnp.where(valid[:, :, None, :], s, -jnp.inf)
        pr = jax.nn.softmax(s, axis=-1)
        return jnp.einsum('bqhk,bqkd->bqhd', pr.astype(v.dtype), v_sel)

    out = lax.map(one_block, (to_blocks(q, nb), to_blocks(q_idx, nb), to_blocks(w_idx, nb), jnp.arange(nb)))
    return from_blocks(out)

def causal_attention(q, k, v):
    B, S, H, Dq = q.shape
    nb = S // Q_BLOCK
    scale = Dq ** -0.5
    kpos = jnp.arange(S)

    def one_block(args):
        qb, i = args
        qpos = i * Q_BLOCK + jnp.arange(Q_BLOCK)
        s = jnp.einsum('bqhd,bkhd->bhqk', qb, k, preferred_element_type=jnp.float32) * scale
        s = jnp.where((kpos[None, :] <= qpos[:, None])[None, None], s, -jnp.inf)
        pr = jax.nn.softmax(s, axis=-1)
        return jnp.einsum('bhqk,bkhd->bqhd', pr.astype(v.dtype), v)

    out = lax.map(one_block, (to_blocks(q, nb), jnp.arange(nb)))
    return from_blocks(out)

def conformer_conv(u, conv_w, conv_b, ln_g, ln_b):
    a, g = jnp.split(u, 2, axis=-1)
    h = a * jax.nn.sigmoid(g)
    h = lax.conv_general_dilated(h, conv_w[:, None, :].astype(h.dtype), window_strides=(1,),
                                 padding=((CONV_W - 1, 0),),
                                 dimension_numbers=('NWC', 'WIO', 'NWC'),
                                 feature_group_count=C_CH) + conv_b
    return jax.nn.silu(layer_norm(h, ln_g, ln_b))

def hybrid_layer(x, p_i, rope_a, rope_b, w_in, b_gate, q_norm_g, w_uq, kv_norm_g, w_ukv,
                 conv_w, conv_b, conv_ln_g, conv_ln_b, w_branch, w_out, ln1_g, ln1_b,
                 w_ffn_in, w_ffn_out, w_ple_gate, w_ple_proj, ln2_g, ln2_b):
    B, S, _ = x.shape
    cos_a, sin_a = rope_a
    cos_b, sin_b = rope_b
    h = x @ w_in
    qa, ka, va, qi, ki, wi, cq, ckv, kr, conv_in, gate_pre = jnp.split(h, IN_SPLITS, axis=-1)

    qa = apply_rope(qa.reshape(B, S, A_HEADS, A_HEAD_DIM), cos_a, sin_a)
    ka = apply_rope(ka, cos_a, sin_a)
    qi = apply_rope(qi.reshape(B, S, IDX_HEADS, IDX_DIM), cos_a, sin_a)
    ki = apply_rope(ki, cos_a, sin_a)
    y_a = dsa_attention(qa, ka, va, qi, ki, wi).reshape(B, S, BRANCH_W)

    qb = (rms_norm(cq, q_norm_g) @ w_uq).reshape(B, S, B_HEADS, B_NOPE + B_ROPE)
    q_nope, q_rope = jnp.split(qb, [B_NOPE], axis=-1)
    q_rope = apply_rope(q_rope, cos_b, sin_b)
    kvb = (rms_norm(ckv, kv_norm_g) @ w_ukv).reshape(B, S, B_HEADS, B_NOPE + B_V)
    k_nope, v_b = jnp.split(kvb, [B_NOPE], axis=-1)
    k_rope = apply_rope(kr, cos_b, sin_b)
    q_full = jnp.concatenate([q_nope, q_rope], axis=-1)
    k_full = jnp.concatenate([k_nope, jnp.broadcast_to(k_rope[:, :, None, :], (B, S, B_HEADS, B_ROPE))], axis=-1)
    y_b = causal_attention(q_full, k_full, v_b).reshape(B, S, BRANCH_W)

    y_c = conformer_conv(conv_in, conv_w, conv_b, conv_ln_g, conv_ln_b)

    gates = jax.nn.sigmoid(gate_pre.reshape(B, S, N_BRANCH, D_MODEL) + b_gate)
    merged = (gates[:, :, 0] * (y_a @ w_branch[0])
              + gates[:, :, 1] * (y_b @ w_branch[1])
              + gates[:, :, 2] * (y_c @ w_branch[2]))
    x = layer_norm(ALPHA * x + merged @ w_out, ln1_g, ln1_b)

    f_gate, f_up = jnp.split(x @ w_ffn_in, 2, axis=-1)
    ffn = (jax.nn.silu(f_gate) * f_up) @ w_ffn_out
    ple = jax.nn.sigmoid(x @ w_ple_gate) * (p_i @ w_ple_proj)
    return layer_norm(ALPHA * x + ffn + ple, ln2_g, ln2_b)

def setup_inputs(seed: int = 0) -> dict:
    key = jax.random.key(seed)
    ks = jax.random.split(key, 24)
    f32 = jnp.float32
    nrm = lambda k, shp, sc: jax.random.normal(k, shp, f32) * sc
    L, D = DEPTH, D_MODEL
    offset = jax.random.randint(ks[2], (BATCH, 1), 0, SEQ, dtype=jnp.int32)
    return {
        "x": nrm(ks[0], (BATCH, SEQ, D), 1.0),
        "p": nrm(ks[1], (DEPTH, BATCH, SEQ, PLE_DIM), 1.0),
        "positions": offset + jnp.arange(SEQ, dtype=jnp.int32)[None, :],
        "w_in": nrm(ks[3], (L, D, N_IN), D ** -0.5),
        "b_gate": nrm(ks[4], (L, N_BRANCH, D), 0.02),
        "q_norm_g": 1.0 + nrm(ks[5], (L, Q_LORA), 0.02),
        "w_uq": nrm(ks[6], (L, Q_LORA, B_HEADS * (B_NOPE + B_ROPE)), Q_LORA ** -0.5),
        "kv_norm_g": 1.0 + nrm(ks[7], (L, KV_LORA), 0.02),
        "w_ukv": nrm(ks[8], (L, KV_LORA, B_HEADS * (B_NOPE + B_V)), KV_LORA ** -0.5),
        "conv_w": nrm(ks[9], (L, CONV_W, C_CH), CONV_W ** -0.5),
        "conv_b": nrm(ks[10], (L, C_CH), 0.02),
        "conv_ln_g": 1.0 + nrm(ks[11], (L, C_CH), 0.02),
        "conv_ln_b": nrm(ks[12], (L, C_CH), 0.02),
        "w_branch": nrm(ks[13], (L, N_BRANCH, BRANCH_W, D), BRANCH_W ** -0.5 * OUT_SCALE),
        "w_out": nrm(ks[14], (L, D, D), D ** -0.5 * OUT_SCALE),
        "ln1_g": 1.0 + nrm(ks[15], (L, D), 0.02),
        "ln1_b": nrm(ks[16], (L, D), 0.02),
        "w_ffn_in": nrm(ks[17], (L, D, 2 * FF), D ** -0.5),
        "w_ffn_out": nrm(ks[18], (L, FF, D), FF ** -0.5 * OUT_SCALE),
        "w_ple_gate": nrm(ks[19], (L, D, D), D ** -0.5),
        "w_ple_proj": nrm(ks[20], (L, PLE_DIM, D), PLE_DIM ** -0.5 * OUT_SCALE),
        "ln2_g": 1.0 + nrm(ks[21], (L, D), 0.02),
        "ln2_b": nrm(ks[22], (L, D), 0.02),
    }

def reference(x, p, positions, w_in, b_gate, q_norm_g, w_uq, kv_norm_g, w_ukv, conv_w, conv_b,
              conv_ln_g, conv_ln_b, w_branch, w_out, ln1_g, ln1_b, w_ffn_in, w_ffn_out,
              w_ple_gate, w_ple_proj, ln2_g, ln2_b):
    rope_a = rope_tables(positions, A_HEAD_DIM)
    rope_b = rope_tables(positions, B_ROPE)
    for i in range(DEPTH):
        x = hybrid_layer(x, p[i], rope_a, rope_b, w_in[i], b_gate[i], q_norm_g[i], w_uq[i],
                         kv_norm_g[i], w_ukv[i], conv_w[i], conv_b[i], conv_ln_g[i], conv_ln_b[i],
                         w_branch[i], w_out[i], ln1_g[i], ln1_b[i], w_ffn_in[i], w_ffn_out[i],
                         w_ple_gate[i], w_ple_proj[i], ln2_g[i], ln2_b[i])
    return x


_drawn_inputs = setup_inputs


def setup_inputs(seed=0):
    import zlib

    import numpy as np

    out = dict(_drawn_inputs(seed))
    spreads = {}
    factors = {'b_gate': 8.0,
     'q_norm_g': 8.0,
     'w_uq': 3.286,
     'kv_norm_g': 8.0,
     'conv_b': 8.0,
     'conv_ln_g': 8.0,
     'conv_ln_b': 8.0}
    for name, (base, spread) in spreads.items():
        noise = np.random.default_rng([zlib.crc32(name.encode()), seed]).standard_normal(out[name].shape)
        drawn = base * np.exp(spread * noise) if base else spread * noise
        out[name] = __import__('jax').numpy.asarray(drawn.astype(out[name].dtype))
    for name, factor in factors.items():
        out[name] = (out[name] * factor).astype(out[name].dtype)
    return out
```

```python
from contextlib import ExitStack

import numpy as np

import concourse.bass as bass
from concourse import mybir

ALU = mybir.AluOpType
ACT = mybir.ActivationFunctionType
F32 = mybir.dt.float32
F32R = mybir.dt.float32r
I32 = mybir.dt.int32

P = 128
D = 1024
S = 512
L = 2
NT = S // P
DK = D // P
PLE = 256
AH, AD = 8, 64
IH, ID = 4, 64
TOPK = min(256, S // 4)
BH, BN, BR, BV = 8, 64, 32, 64
BQ = BN + BR
QL, KVL = 384, 256
CC, CW = 512, 31
CK = CC // P
FF = (8 * D + 3 * 256 - 1) // (3 * 256) * 256
FK = FF // P
THETA = 10000.0
LN_EPS, RMS_EPS = 1e-5, 1e-6
ALPHA = float((2 * L) ** 0.25)
assert TOPK == P

C_QA = 0
C_KA = C_QA + AH * AD
C_VA = C_KA + AD
C_QI = C_VA + AD
C_KI = C_QI + IH * ID
C_WI = C_KI + ID
C_CQ = C_WI + IH
C_CKV = C_CQ + QL
C_KR = C_CKV + KVL
C_CA = C_KR + BR
C_CG = C_CA + CC
C_GATE = C_CG + CC
N_IN = C_GATE + 3 * D

NEG = -1e30
TAKEN = -3e38

TOKEN_GROUPS = [("idx", 452, 2, 4), ("cq", 416, 2, 4), ("ckv", 256, 4, 2), ("qa", 512, 2, 4)]
TOKEN_GROUPS += [("uq", 192, 3, 1)] * 4 + [("ukv", 512, 2, 1)] * 2
G_KI, G_KA, G_VA, G_WI = 256, 320, 384, 448

T_CONV = 14
T_U = T_CONV + 2 * CK
T_GA = T_U + 6
T_GB = T_GA + DK
T_GC = T_GB + DK
T_BR = T_GC + DK
T_OUT = T_BR + 12
T_PP = T_OUT + DK
T_PG = T_PP + 2
T_FI = T_PG + DK
T_FO = T_FI + 2 * FK
TILES = T_FO + FK
assert TILES % 4 == 0
TILE = 1024
LEAD = 3
WS = 4
START = 1

PAR, _at = {}, 0
for _n, _c in (("bg", 3 * DK), ("cw", CK * CW), ("gq", 3), ("gkv", 2), ("cb", CK), ("clg", CK), ("clb", CK),
               ("l1g", DK), ("l1b", DK), ("l2g", DK), ("l2b", DK)):
    PAR[_n] = _at
    _at += _c
NPAR = _at
HALVED = PAR["gq"]

HEADS = 4
UNITS = HEADS * NT


def attention_steps(prep_units):
    left = [(t, k) for t in range(4) for k in range(DK)]
    steps = []

    def parts(n):
        for _ in range(n):
            steps.append(("part", left.pop(0)))

    parts(1)
    steps.append(("prep", 0))
    parts(1)
    for s in range(UNITS):
        steps.append(("score", s))
        parts(0 if s % NT == 0 else 1)
        if s >= 1:
            steps.append(("turn", s - 1))
        parts(1)
        if s >= 2:
            steps.append(("value", s - 2))
        if s % prep_units == 1 and s + prep_units < UNITS:
            steps.append(("prep", s // prep_units + 1))
    steps.append(("turn", UNITS - 1))
    steps.append(("value", UNITS - 2))
    steps.append(("value", UNITS - 1))
    parts(2)
    steps += [("out", 0), ("out", 1)]
    assert not left
    return steps


def scalar_steps(steps):
    order = []
    for kind, n in steps:
        if kind == "part":
            if n[1] == 0:
                order.append(("high", n[0]))
            elif n[1] == DK - 1:
                order.append(("gate", n[0]))
        elif kind == "turn" and ("score", n + 1) in order:
            order.insert(order.index(("score", n + 1)), (kind, n))
        else:
            order.append((kind, n))
    return order


STEPS_B = attention_steps(NT)
STEPS_A = attention_steps(2 * NT)
TURNS_B = 2 * HEADS + UNITS + 2
TURNS_A = HEADS // 2 + UNITS + 2
TURNS = 2 * (TURNS_B + TURNS_A)
PAIRS = AH * NT + BH * NT

SCRATCH_T = 9
SCRATCH = SCRATCH_T + IH * (NT - 1)
FRONT = [("tile", t) for t in range(T_CONV)] + [("scratch", n) for n in range(4)] + [("tile", T_CONV)]
FRONT += [("scratch", n) for n in range(4, SCRATCH_T)] + [("tile", T_CONV + 1)]
for _q in range(NT - 1):
    FRONT += [("scratch", SCRATCH_T + IH * _q + _h) for _h in range(IH)] + [("tile", T_CONV + 2 + _q)]
FRONT += [("tile", t) for t in range(T_CONV + NT + 1, T_GA)]

V_FRONT, V_ATTN_B, V_ATTN_A, V_CONV, V_BRANCH, V_OUT, V_LN, V_PG, V_FI = 134, 46, 46, 5, 8, 4, 9, 8, 2
VS_B = V_FRONT
VS_A = VS_B + 2 * V_ATTN_B
VS_CONV = VS_A + 2 * V_ATTN_A
VS_BRANCH = VS_CONV + V_CONV
VS_OUT = VS_BRANCH + V_BRANCH
VS_LN1 = VS_OUT + 2 * V_OUT
VS_PG = VS_LN1 + V_LN
VS_FI = VS_PG + 2 * V_PG
VS_LN2 = VS_FI + FK // 2 * V_FI
V_LAYER = VS_LN2 + V_LN


class Steps:

    def __init__(self, engine, semaphore):
        self.engine, self.semaphore, self.base, self.n = engine, semaphore, 0, 0

    def stage(self, base):
        self.base, self.n = base, 0

    def done(self, instruction):
        instruction.then_inc(self.semaphore, 1)
        self.n += 1

    def wait(self, back=0):
        self.engine.wait_ge(self.semaphore, self.base + (self.n - back))

    def end(self, name, n):
        assert self.n == n, f"{name} has {self.n} steps"


def build(nc, x_t, ple_t, pos, freq, weights, params, out):
    with ExitStack() as ctx:
        BASE = 16512

        def sb(name, offset, shape, dt=F32):
            return nc.alloc_sbuf_tensor_at("sb_" + name, shape, dt, offset=BASE + offset)

        def sem(name):
            return ctx.enter_context(nc.semaphore(name))

        xh = sb("xh", 0, [P, DK, S], F32R)
        xl = sb("xl", 16384, [P, DK, S], F32R)
        wraw = sb("wraw", 32768, [P, 2, TILE])
        wh = sb("wh", 40960, [P, WS, TILE], F32R)
        wl = sb("wl", 57344, [P, WS, TILE], F32R)
        ident = sb("ident", 73728, [P, P])
        ones_d = sb("ones_d", 74240, [P, P])
        ones_c = sb("ones_c", 74752, [P, P])
        causal = sb("causal", 75264, [P, S])
        cos = sb("cos", 77312, [P, NT, 48])
        sin = sb("sin", 78080, [P, NT, 48])
        par = sb("par", 78848, [P, NPAR])
        praw = sb("praw", 79680, [P, 2, S])
        small = sb("small", 83776, [P, 256])
        A0 = 84800
        h_idx = sb("h_idx", A0 + 0, [P, NT, 452])
        h_qa = sb("h_qa", A0 + 7232, [P, NT, 512])
        h_cq = sb("h_cq", A0 + 15424, [P, NT, 416])
        h_ckv = sb("h_ckv", A0 + 22080, [P, NT, 256])
        conv = sb("conv", A0 + 17984, [P, CK, S])
        uq = sb("uq", A0 + 26176, [P, NT, BH * BQ])
        ukv = sb("ukv", A0 + 38464, [P, NT, BH * (BN + BV)])
        keep_bias = sb("keep_bias", A0 + 54848, [P, 1152])
        hconv = sb("hconv", A0 + 59456, [P, CK, CW - 1 + S])
        ga = sb("ga", A0 + 68128, [P, DK, S])
        ch = sb("ch", A0 + 68128, [P, 5, S], F32R)
        cl = sb("cl", A0 + 78368, [P, 5, S], F32R)
        yb = sb("yb", A0 + 84512, [P, 4, S])
        pbuf = sb("pbuf", A0 + 92704, [P, 2, S])
        ptbuf = sb("ptbuf", A0 + 96800, [P, 2, S])
        qt_buf = sb("qt_buf", A0 + 100896, [P, 2, S])
        kt_buf = sb("kt_buf", A0 + 104992, [P, 2, S])
        stage_q = sb("stage_q", A0 + 109088, [P, 2, NT, BQ])
        stage_k = sb("stage_k", A0 + 112160, [P, 2, NT, BQ])
        stage_a = sb("stage_a", A0 + 109088, [P, 2, NT, P])
        ystage = sb("ystage", A0 + 115232, [P, NT, HEADS * AD])
        work = sb("work", A0 + 92704, [P, 1152])
        scores = sb("scores", A0 + 119328, [P, 1152])
        qi_t = sb("qi_t", A0 + 101920, [P, 2, S])
        ki_t = sb("ki_t", A0 + 106016, [P, S])
        relu = sb("relu", A0 + 108064, [P, 2, S])
        th_conv = sb("th_conv", A0 + 112160, [P, 2, S])
        kdup = sb("kdup", A0 + 112160, [P, 2, NT, P])
        rope_tmp = sb("rope_tmp", A0 + 119328, [P, 3, 512])
        ka_t = sb("ka_t", A0 + 125472, [P, S])
        gb = sb("gb", A0 + 38464, [P, DK, S])
        ya = sb("ya", A0 + 26176, [P, 4, S])
        gc = sb("gc", A0 + 92704, [P, DK, S])
        csq = sb("csq", A0 + 109088, [P, CK, S])
        rstd_c = sb("rstd_c", A0 + 34368, [P, S])
        th_z = [sb("th_z0", A0 + 36416, [P, S]), sb("th_z1", A0 + 125472, [P, S])]
        tmp = sb("tmp", A0 + 36416, [P, S])
        yh = [sb("yah", A0 + 54848, [P, 4, S], F32R), sb("ybh", A0 + 0, [P, 4, S], F32R),
              sb("ych", A0 + 109088, [P, 4, S], F32R)]
        yl = [sb("yal", A0 + 117280, [P, 4, S], F32R), sb("ybl", A0 + 8192, [P, 4, S], F32R),
              sb("ycl", A0 + 84512, [P, 4, S], F32R)]
        msum = sb("msum", A0 + 63040, [P, 2, S])
        mh = sb("mh", A0 + 17984, [P, DK, S], F32R)
        ml = sb("ml", A0 + 68128, [P, DK, S], F32R)
        hh = sb("hh", A0 + 0, [P, FK, S], F32R)
        hl = sb("hl", A0 + 45056, [P, FK, S], F32R)
        u = sb("u", A0 + 90112, [P, DK, S])
        pp = sb("pp", A0 + 106496, [P, DK, S])
        th = sb("th", A0 + 122880, [P, 2, S])
        ph = sb("ph", A0 + 0, [P, 2, S], F32R)
        pl = sb("pl", A0 + 4096, [P, 2, S], F32R)
        rstd = sb("rstd", A0 + 8192, [P, S])
        sq = sb("sq", A0 + 10240, [P, 2, S])
        nmax = small[:, 0:2]
        psums = small[:, 2:6]
        rinv = small[:, 6:8]
        ssq = small[:, 8:16]
        rms = small[:, 16:24]
        eps_ln = small[:, 24:25]
        zero1 = small[:, 25:26]
        posf = small[:, 26:30]
        wi_half = small[:, 32:48].rearrange("p (t h) -> p t h", t=NT)
        top8 = small[:, 48:72]
        posi = small[:, 72:76].bitcast(I32)
        key_rope = small[:, 128:256].rearrange("p (t r) -> p t r", t=NT)

        psum = ctx.enter_context(nc.psum_tensor("banks", [P, 8, 512], F32))

        raw_loaded = [sem("raw_loaded0"), sem("raw_loaded1")]
        hi_ready, lo_ready, tile_used = sem("hi_ready"), sem("lo_ready"), sem("tile_used")
        x_loaded = [sem(f"x_loaded{j}") for j in range(4)]
        consts_ready, zeroed, tables_in, angles, tables, angle_step = (
            sem("consts_ready"), sem("zeroed"), sem("tables_in"), sem("angles"), sem("tables"),
            sem("angle_step"))
        par_loaded, ple_loaded, out_stored = sem("par_loaded"), sem("ple_loaded"), sem("out_stored")
        group_out, roped_idx, dup_ready, ssq_ready, var_rms, sd_rms, normed_c = (
            sem("group_out"), sem("roped_idx"), sem("dup_ready"), sem("ssq_ready"), sem("var_rms"), sem("sd_rms"),
            sem("normed_c"))
        roped_q, roped_u = sem("roped_q"), sem("roped_u")
        scratch_ready, scratch_act, c_low, scored = (
            sem("scratch_ready"), sem("scratch_act"), sem("c_low"), sem("scored"))
        conv_th, conv_in = sem("conv_th"), sem("conv_in")
        staged, score_ready, masked, prob_ready, turned, turn_out, value_ready, value_out = (
            sem("staged"), sem("score_ready"), sem("masked"), sem("prob_ready"), sem("turned"), sem("turn_out"),
            sem("value_ready"), sem("value_out"))
        gate_done = sem("gate_done")
        conv_done, stat_ready, centered_c, squared_c, sd_c, z_conv, th_ready, y2_ready = (
            sem("conv_done"), sem("stat_ready"), sem("centered_c"), sem("squared_c"), sem("sd_c"), sem("z_conv"),
            sem("th_ready"), sem("y2_ready"))
        y_high, y_low, branch_out, merged, merged_high, merged_low = (
            sem("y_high"), sem("y_low"), sem("branch_out"), sem("merged"), sem("merged_high"), sem("merged_low"))
        u_ready, mean_ready, centered, squared, var_step, sd_ready, z_ready, x_high, x_ready = (
            sem("u_ready"), sem("mean_ready"), sem("centered"), sem("squared"), sem("var_step"), sem("sd_ready"),
            sem("z_ready"), sem("x_high"), sem("x_ready"))
        p_high, p_low, pp_out, ple_th, h_done, ffn_th, ffn_s, ffn_high, ffn_out = (
            sem("p_high"), sem("p_low"), sem("pp_out"), sem("ple_th"), sem("h_done"), sem("ffn_th"), sem("ffn_s"),
            sem("ffn_high"), sem("ffn_out"))
        vec = sem("vec")
        passed = sem("passed")

        def width(qt):
            return (qt + 1) * P

        def wide(qt):
            return sum(width(q) for q in range(1, qt))

        def column(name, j):
            return par[:, PAR[name] + j:PAR[name] + j + 1]

        block = ctx.enter_context(nc.Block())

        @block.sync
        def _(sp):
            for t in range(2):
                sp.dma_start(wraw[:, t, :], weights[t]).then_inc(raw_loaded[t], 16)
            with sp.Fori(1, L * TILES // 2) as m:
                for t in range(2):
                    sp.wait_ge(lo_ready, m * 2 + (t - 1))
                    sp.dma_start(wraw[:, t, :], weights[bass.ds(m * 2 + t, 1)].rearrange("a p n -> (a p) n")).then_inc(
                        raw_loaded[t], 16)

        @block.gpsimd
        def _(pool):
            nc.gpsimd.memset(ident[:], 0.0).then_inc(zeroed, 1)
            nc.gpsimd.memset(causal[:], 0.0).then_inc(zeroed, 1)
            nc.gpsimd.memset(ones_d[:], 1.0 / D).then_inc(consts_ready, 1)
            nc.gpsimd.memset(ones_c[:], 1.0 / CC).then_inc(consts_ready, 1)
            nc.gpsimd.memset(eps_ln, LN_EPS).then_inc(consts_ready, 1)
            pool.wait_ge(zeroed, 2)
            nc.gpsimd.affine_select(out=ident[:], in_=ident[:], compare_op=ALU.not_equal, fill=1.0, base=0,
                                    pattern=[[-1, P]], channel_multiplier=1).then_inc(consts_ready, 1)
            nc.gpsimd.affine_select(out=causal[:, S - P:S], in_=causal[:, S - P:S], compare_op=ALU.is_ge, fill=NEG,
                                    base=0, pattern=[[-1, P]], channel_multiplier=1).then_inc(consts_ready, 1)

            def low(t, first):
                pool.wait_ge(hi_ready, first + (t + 1))
                nc.gpsimd.tensor_tensor(wl[:, t % WS, :], wraw[:, t % 2, :], wh[:, t % WS, :].bitcast(F32),
                                        ALU.subtract).then_inc(lo_ready, 1)

            def stage(mixer, i, layer, h):
                if mixer == "B":
                    per, uses, first = HEADS, STEPS_B, 0
                else:
                    per, uses, first = HEADS // 2, STEPS_A, 2 * TURNS_B
                per_body = TURNS_B if mixer == "B" else TURNS_A
                seen, turns = 0, 0
                for kind, n in uses:
                    if h >= 2 and seen == h - 1:
                        break
                    if kind == "prep":
                        seen += 1
                        turns += 2 if mixer == "B" else 1
                    if kind in ("turn", "out"):
                        turns += 1
                need = turns if h >= 2 else 0
                pool.wait_ge(turned, layer * TURNS + first + i * per_body + (need + START))
                if mixer == "B":
                    q = uq[:, :, bass.ds(i * (HEADS * BQ) + h * BQ, BQ)]
                    k = ukv[:, :, bass.ds(i * (HEADS * P) + h * P, BN)]
                    nc.gpsimd.tensor_copy(stage_q[:, h % 2], q).then_inc(staged, 1)
                    nc.gpsimd.tensor_copy(stage_k[:, h % 2, :, 0:BN], k).then_inc(staged, 1)
                    nc.gpsimd.tensor_copy(stage_k[:, h % 2, :, BN:BQ], key_rope).then_inc(staged, 1)
                else:
                    q = h_qa[:, :, bass.ds(i * (HEADS * AD) + h * P, P)]
                    nc.gpsimd.tensor_copy(stage_a[:, h % 2], q).then_inc(staged, 1)

            with pool.Fori(0, L) as layer:
                first = layer * TILES
                for t in range(LEAD):
                    low(t, first)
                with pool.Fori(0, T_GA // 4) as i:
                    for k in range(4):
                        low(LEAD + k, first + i * 4)
                pool.wait_ge(roped_u, layer * 2 + 2)
                pool.wait_ge(group_out, layer * 40 + 40)
                pool.wait_ge(conv_in, layer * CK + CK)
                pool.sem_inc(passed, 1)
                with pool.Fori(0, 2) as i:
                    stage("B", i, layer, 0)
                    stage("B", i, layer, 1)
                    for k in range(4):
                        low(T_GA + LEAD + k, first + i * 4)
                        if k < HEADS - 2:
                            stage("B", i, layer, k + 2)
                pool.wait_ge(roped_q, layer * 2 + 2)
                pool.sem_inc(passed, 1)
                with pool.Fori(0, 2) as i:
                    stage("A", i, layer, 0)
                    stage("A", i, layer, 1)
                    for k in range(4):
                        low(T_GB + LEAD + k, first + i * 4)
                rest = T_GC + LEAD
                with pool.Fori(0, (TILES - rest) // 4) as i:
                    for k in range(4):
                        low(rest + k, first + i * 4)
                for t in range(rest + (TILES - rest) // 4 * 4, TILES):
                    low(t, first)


        def logit(n):
            k = n - SCRATCH_T
            return NT - 1 - k // IH, k % IH

        tile_group, t, col = {}, 0, {}
        for g, (name, ncol, nk, tiles) in enumerate(TOKEN_GROUPS):
            col[g] = sum(n for gg, (nm, n, _, _) in enumerate(TOKEN_GROUPS) if gg < g and nm == name)
            for k in range(tiles):
                tile_group[t] = (g, k)
                t += 1
            if t == T_CONV:
                t = T_U
        group_dst = {"idx": h_idx, "cq": h_cq, "ckv": h_ckv, "qa": h_qa, "uq": uq, "ukv": ukv}

        @block.scalar
        def _(act):
            act.dma_start(posi, pos).then_inc(tables_in, 16)
            act.dma_start(rope_tmp[:, 0, 0:48], freq).then_inc(tables_in, 16)
            for j in range(4):
                act.dma_start(u[:, 2 * j:2 * j + 2], x_t[:, 2 * j:2 * j + 2]).then_inc(x_loaded[j], 16)
            act.sem_inc(ple_th, 2)
            for s in (gate_done, turn_out, ssq_ready):
                act.sem_inc(s, START)
            act.sem_inc(out_stored, 16 * START)
            act.wait_ge(angles, 2)
            nc.scalar.activation(sin[:], rope_tmp[:, 1, 0:192], ACT.Sin).then_inc(tables, 1)
            nc.scalar.activation(cos[:], rope_tmp[:, 2, 0:192], ACT.Sin).then_inc(tables, 1)
            for j in range(DK):
                if j % 2 == 0:
                    act.wait_ge(x_loaded[j // 2], 16)
                nc.scalar.activation(xh[:, j], u[:, j], ACT.Copy).then_inc(x_high, 1)
            act.wait_ge(consts_ready, 5)

            def high(t, first):
                act.wait_ge(tile_used, first + (max(t - (WS - 1), 0) + START))
                act.wait_ge(raw_loaded[t % 2], first * 8 + 16 * (t // 2 + 1))
                nc.scalar.activation(wh[:, t % WS, :], wraw[:, t % 2, :], ACT.Copy).then_inc(hi_ready, 1)

            def gate(t, first, bank, dst, bias, done):
                act.wait_ge(tile_used, first + (t + 1 + START))
                nc.scalar.activation(dst, psum[:, bank, :], ACT.Tanh, scale=0.5, bias=bias).then_inc(done, 1)

            def attention(mixer, layer, first):
                steps, per_body, t0 = (STEPS_B, TURNS_B, T_GA) if mixer == "B" else (STEPS_A, TURNS_A, T_GB)
                u0, r0 = (0, 0) if mixer == "B" else (BH * NT, 2 * TURNS_B)
                dst, y, g0 = (ga, yb, 0) if mixer == "B" else (gb, ya, DK)
                heads = 1 if mixer == "B" else 2
                order = scalar_steps(steps)
                with act.Fori(0, 2) as i:
                    unit = layer * PAIRS + i * UNITS + u0
                    turn = layer * TURNS + i * per_body + r0
                    r = 0

                    def turned_out(out, rows, w):
                        nonlocal r
                        act.wait_ge(turned, turn + (r + 1 + START))
                        nc.scalar.activation(out, psum[0:rows, 2 + r % 2, 0:w], ACT.Copy).then_inc(turn_out, 1)
                        r += 1

                    for kind, n in order:
                        if kind == "high":
                            high(t0 + n + LEAD, first + i * 4)
                        elif kind == "gate":
                            b = par[:, bass.ds(i * 4 + (PAR["bg"] + g0 + n), 1)]
                            o = dst[:, bass.ds(i * 4 + n, 1), :].rearrange("p a n -> p (a n)")
                            gate(t0 + n, first + i * 4, 6 + n % 2, o, b, gate_done)
                        elif kind == "prep":
                            act.wait_ge(score_ready, unit + (max(heads * NT * (n - 1), 0) + START))
                            if mixer == "B":
                                turned_out(qt_buf[0:BQ, n % 2, :], BQ, S)
                                turned_out(kt_buf[0:BQ, n % 2, :], BQ, S)
                            else:
                                turned_out(qt_buf[:, n % 2, :], P, S)
                        elif kind == "turn":
                            act.wait_ge(value_ready, unit + (max(n - 1, 0) + START))
                            turned_out(ptbuf[:, n % 2, 0:width(n % NT)], P, width(n % NT))
                        elif kind == "score":
                            w = width(n % NT)
                            act.wait_ge(masked, unit + (n + 1 + START))
                            nc.scalar.activation(pbuf[:, n % 2, 0:w], pbuf[:, n % 2, 0:w], ACT.Exp, scale=-1.0,
                                                 bias=nmax[:, n % 2:n % 2 + 1],
                                                 accum_out=psums[:, n % 4:n % 4 + 1]).then_inc(prob_ready, 1)
                        elif kind == "out":
                            turned_out(y[:, bass.ds(i * 2 + n, 1), :].rearrange("p a n -> p (a n)"), P, S)

            def norm(layer, n, between):
                x0 = layer * 16 + 8 * n
                for j in range(DK):
                    act.wait_ge(centered, x0 + (j + 1))
                    if j >= 2:
                        act.wait_ge(var_step, x0 + (j - 1))
                    nc.scalar.activation(sq[:, j % 2], u[:, j], ACT.Square).then_inc(squared, 1)
                between()
                act.wait_ge(var_step, x0 + DK)
                nc.scalar.activation(rstd[:], psum[:, 1, :], ACT.Sqrt, bias=eps_ln).then_inc(sd_ready, 1)

            def norm_high(layer, n):
                x0 = layer * 16 + 8 * n
                for j in range(DK):
                    act.wait_ge(z_ready, x0 + (j + 1))
                    nc.scalar.activation(xh[:, j], u[:, j], ACT.Copy).then_inc(x_high, 1)

            with act.Fori(0, L) as layer:
                first = layer * TILES
                for t in range(LEAD):
                    high(t, first)
                act.wait_ge(x_ready, layer * 16 + DK)
                act.dma_start(par[:], params[bass.ds(layer, 1)].rearrange("a p n -> (a p) n")).then_inc(par_loaded, 16)
                act.dma_start(praw[:], ple_t[bass.ds(layer, 1)].rearrange("a p k n -> (a p) k n")).then_inc(
                    ple_loaded, 16)
                for kind, n in FRONT:
                    if kind == "tile":
                        high(n + LEAD, first)
                        if n in tile_group:
                            g, k = tile_group[n]
                            name, ncol, _, tiles = TOKEN_GROUPS[g]
                            if k == tiles - 1:
                                act.wait_ge(tile_used, first + (n + 1 + START))
                                for b in range(NT):
                                    nc.scalar.activation(group_dst[name][:, b, col[g]:col[g] + ncol],
                                                         psum[:, 4 * (g % 2) + b, 0:ncol],
                                                         ACT.Copy).then_inc(group_out, 1)
                        elif n >= T_CONV and (n - T_CONV) % 2 == 0:
                            j = (n - T_CONV) // 2
                            if j >= 2:
                                act.wait_ge(conv_in, layer * CK + (j - 1))
                            gate(n, first, 6, th_conv[:, j % 2, :], 0.0, conv_th)
                        if n == 5:
                            act.wait_ge(roped_idx, layer * 2 + 2)
                            for w, c in ((0, G_KI), (1, G_KA)):
                                src = h_idx[:, :, c:c + AD].unsqueeze(2).to_broadcast([P, NT, 2, AD])
                                nc.scalar.activation(kdup[:, w].rearrange("p t (r d) -> p t r d", r=2), src,
                                                     ACT.Copy).then_inc(dup_ready, 1)
                        if n in (7, 9):
                            src, c, nn = (h_cq, QL, 0) if n == 7 else (h_ckv, KVL, NT)
                            for b in range(NT):
                                act.wait_ge(group_out, layer * 40 + (8 if n == 7 else 12))
                                act.wait_ge(ssq_ready, layer * 8 + (nn + b + START))
                                nc.scalar.activation(relu[:, 0, 0:c], src[:, b, 0:c], ACT.Square,
                                                     accum_out=ssq[:, nn + b:nn + b + 1]).then_inc(ssq_ready, 1)
                        if n == 11:
                            act.wait_ge(var_rms, layer * 2 + 2)
                            nc.scalar.activation(rms, rms, ACT.Sqrt).then_inc(sd_rms, 1)
                    else:
                        bank = n % 4
                        act.wait_ge(scratch_ready, layer * SCRATCH + (n + 1))
                        if n < 4:
                            dst = (qi_t[:, 0], qi_t[:, 1], ki_t[:], ka_t[:])[n]
                            nc.scalar.activation(dst, psum[:, bank, :], ACT.Copy).then_inc(scratch_act, 1)
                        elif n < SCRATCH_T:
                            if n == 4:
                                act.wait_ge(par_loaded, layer * 16 + 16)
                            nc.scalar.activation(ch[:, n - 4], psum[:, bank, :], ACT.Copy,
                                                 scale=column("gq", n - 4)).then_inc(scratch_act, 1)
                        else:
                            k, w = n - SCRATCH_T, width(logit(n)[0])
                            if k >= 2:
                                act.wait_ge(scored, layer * 12 + (k - 1))
                            nc.scalar.activation(relu[:, k % 2, 0:w], psum[:, bank, 0:w], ACT.Relu,
                                                 scale=ID ** -0.5).then_inc(scratch_act, 1)
                attention("B", layer, first)
                attention("A", layer, first)

                act.wait_ge(turn_out, layer * TURNS + (TURNS + START))
                act.wait_ge(masked, layer * PAIRS + (PAIRS + START))
                act.wait_ge(conv_done, layer * CK + CK)
                nc.scalar.activation(yh[1][:], yb[:], ACT.Copy).then_inc(y_high, 1)
                nc.scalar.activation(yh[0][:], ya[:], ACT.Copy).then_inc(y_high, 1)
                for k in range(DK):
                    t = T_GC + k
                    high(t + LEAD, first)
                    gate(t, first, 6 + k % 2, gc[:, k], column("bg", 2 * DK + k), gate_done)
                    if k == 0:
                        for j in range(CK):
                            act.wait_ge(centered_c, layer * CK + (j + 1))
                            nc.scalar.activation(csq[:, j], conv[:, j], ACT.Square).then_inc(squared_c, 1)
                    if k == 5:
                        act.wait_ge(stat_ready, layer * 2 + 2)
                        nc.scalar.activation(rstd_c[:], psum[:, 1, :], ACT.Sqrt, bias=eps_ln).then_inc(sd_c, 1)
                for j in range(CK + 1):
                    if j < CK:
                        act.wait_ge(z_conv, layer * CK + (j + 1))
                        if j >= 2:
                            act.wait_ge(y2_ready, layer * CK + (j - 1))
                        nc.scalar.activation(th_z[j % 2][:], conv[:, j], ACT.Tanh, scale=0.5).then_inc(th_ready, 1)
                    if j >= 1:
                        act.wait_ge(y2_ready, layer * CK + j)
                        nc.scalar.activation(yh[2][:, j - 1], conv[:, j - 1], ACT.Copy, scale=0.5).then_inc(y_high, 1)
                for q in range(12):
                    high(T_BR + q + LEAD, first)
                    if q % 3 == 2:
                        for c in range(2):
                            n = 2 * (q // 3) + c
                            act.wait_ge(merged, layer * DK + (n + 1))
                            nc.scalar.activation(mh[:, n], msum[:, c], ACT.Copy, scale=0.5).then_inc(merged_high, 1)
                act.wait_ge(ple_loaded, layer * 16 + 16)
                act.wait_ge(tile_used, first + (T_OUT + START))
                nc.scalar.activation(ph[:], praw[:], ACT.Copy).then_inc(p_high, 1)
                with act.Fori(0, 2) as i:
                    for k in range(4):
                        high(T_OUT + k + LEAD, first + i * 4)

                def embedding_out(q):
                    act.wait_ge(tile_used, first + (T_PP + q + 1 + START))
                    for c in range(4):
                        nc.scalar.activation(pp[:, 4 * q + c], psum[:, 2 + c, :], ACT.Copy,
                                             scale=0.5).then_inc(pp_out, 1)

                def between():
                    embedding_out(0)
                    high(T_PP + 1 + LEAD, first)

                high(T_PP + LEAD, first)
                norm(layer, 0, between)
                embedding_out(1)
                norm_high(layer, 0)
                with act.Fori(0, 2) as i:
                    for k in range(4):
                        high(T_PG + k + LEAD, first + i * 4)
                        act.wait_ge(h_done, layer * (DK + FK) + i * 4 + (k + 1))
                        gate(T_PG + k, first + i * 4, 6 + k % 2, th[:, k % 2, :], 0.0, ple_th)
                with act.Fori(0, FK // 2) as i:
                    for c in range(2):
                        high(T_FI + 2 * c + LEAD, first + i * 4)
                        act.wait_ge(h_done, layer * (DK + FK) + i * 2 + (DK + c + 1))
                        gate(T_FI + 2 * c, first + i * 4, 4 + 2 * c, th[:, c, :], 0.0, ffn_th)
                        high(T_FI + 2 * c + 1 + LEAD, first + i * 4)
                        act.wait_ge(ffn_s, layer * FK + i * 2 + (c + 1))
                        nc.scalar.activation(hh[:, bass.ds(i * 2 + c, 1), :].rearrange("p a n -> p (a n)"),
                                             th[:, c, :], ACT.Copy, scale=0.5).then_inc(ffn_high, 1)
                left = TILES - T_FO - LEAD
                with act.Fori(0, left // 4) as i:
                    for k in range(4):
                        high(T_FO + LEAD + k, first + i * 4)
                for t in range(T_FO + LEAD + left // 4 * 4, TILES):
                    high(t, first)
                norm(layer, 1, lambda: None)
                norm_high(layer, 1)
                act.dma_start(out[bass.ds(layer, 1)].rearrange("a p k n -> (a p) k n"), u[:]).then_inc(out_stored, 16)
            act.wait_ge(out_stored, 16 * (L + START))

        @block.tensor
        def _(pe):
            def three(out, wh_, wl_, xh_, xl_, start, stop):
                nc.tensor.matmul(out, wh_, xh_, start=start, stop=False)
                nc.tensor.matmul(out, wh_, xl_, start=False, stop=False)
                return nc.tensor.matmul(out, wl_, xh_, start=False, stop=stop)

            def arrived(t, first):
                pe.wait_ge(lo_ready, first + (t + 1))

            def project(t, first, src_h, src_l, nk, outs, ready=None):
                arrived(t, first)
                n = len(outs) * P
                h = wh[:, t % WS, 0:nk * n].rearrange("p (k n) -> p k n", k=nk)
                lw = wl[:, t % WS, 0:nk * n].rearrange("p (k n) -> p k n", k=nk)
                for c, bank in enumerate(outs):
                    for k in range(nk):
                        if ready is not None and c == 0:
                            ready(k)
                        last = three(psum[:, bank, :], h[:, k, c * P:c * P + P], lw[:, k, c * P:c * P + P],
                                     src_h[:, k], src_l[:, k], k == 0, k == nk - 1)
                last.then_inc(tile_used, 1)

            def group(t, layer, first):
                g, part = tile_group[t]
                name, ncol, nk, tiles = TOKEN_GROUPS[g]
                if part == 0:
                    if g >= 2:
                        pe.wait_ge(group_out, layer * 40 + 4 * (g - 1))
                    if g == 4:
                        pe.wait_ge(scratch_act, layer * SCRATCH + SCRATCH)
                        pe.wait_ge(c_low, layer * 5 + 5)
                    if g == 5:
                        pe.wait_ge(conv_in, layer * CK + CK)
                arrived(t, first)
                src_h, src_l, k0 = (xh, xl, 0) if g < 4 else (ch, cl, 0 if name == "uq" else 3)
                h = wh[:, t % WS, 0:nk * ncol].rearrange("p (k n) -> p k n", k=nk)
                lw = wl[:, t % WS, 0:nk * ncol].rearrange("p (k n) -> p k n", k=nk)
                for kk in range(nk):
                    k = nk * part + kk
                    if g == 0:
                        pe.wait_ge(x_ready, layer * 16 + (k + 1))
                    for b in range(NT):
                        o = psum[:, 4 * (g % 2) + b, 0:ncol]
                        th_, tl_ = src_h[:, k0 + k, b * P:b * P + P], src_l[:, k0 + k, b * P:b * P + P]
                        nc.tensor.matmul(o, th_, h[:, kk], start=(k == 0), stop=False)
                        nc.tensor.matmul(o, th_, lw[:, kk], start=False, stop=False)
                        last = nc.tensor.matmul(o, tl_, h[:, kk], start=False, stop=(k == nk * tiles - 1))
                last.then_inc(tile_used, 1)

            def scratch(n, layer):
                if n >= 4:
                    pe.wait_ge(scratch_act, layer * SCRATCH + (n - 3))
                if 4 <= n - 4 < SCRATCH_T:
                    pe.wait_ge(c_low, layer * 5 + (n - 7))
                if n == 0:
                    pe.wait_ge(group_out, layer * 40 + 12)
                    pe.wait_ge(roped_idx, layer * 2 + 2)
                if n == 2:
                    pe.wait_ge(dup_ready, layer * 2 + 2)
                if n == 4:
                    pe.wait_ge(normed_c, layer * 8 + 8)
                if n < SCRATCH_T:
                    for b in range(NT):
                        if n < 2:
                            src = h_idx[:, b, n * P:n * P + P]
                        elif n < 4:
                            src = kdup[:, n - 2, b]
                        elif n < 7:
                            src = h_cq[:, b, (n - 4) * P:(n - 4) * P + P]
                        else:
                            src = h_ckv[:, b, (n - 7) * P:(n - 7) * P + P]
                        last = nc.tensor.transpose(psum[:, n % 4, b * P:b * P + P], src, ident[:])
                else:
                    qt, h = logit(n)
                    rows = slice(ID * (h % 2), ID * (h % 2) + ID)
                    last = nc.tensor.matmul(psum[:, n % 4, 0:width(qt)], qi_t[rows, h // 2, qt * P:qt * P + P],
                                            ki_t[rows, 0:width(qt)], start=True, stop=True)
                last.then_inc(scratch_ready, 1)

            def attention(mixer, layer, first):
                steps, per_body, t0 = (STEPS_B, TURNS_B, T_GA) if mixer == "B" else (STEPS_A, TURNS_A, T_GB)
                u0, r0, g0 = (0, 0, 0) if mixer == "B" else (BH * NT, 2 * TURNS_B, DK)
                with pe.Fori(0, 2) as i:
                    unit = layer * PAIRS + i * UNITS + u0
                    turn = layer * TURNS + i * per_body + r0
                    r, ready_at, turn_at = 0, {}, {}

                    def turn_blocks(blocks, rows):
                        nonlocal r
                        pe.wait_ge(turn_out, turn + (max(r - 1, 0) + START))
                        for b, src in enumerate(blocks):
                            last = nc.tensor.transpose(psum[0:rows, 2 + r % 2, b * P:b * P + P], src, ident[:])
                        last.then_inc(turned, 1)
                        r += 1

                    for kind, n in steps:
                        if kind == "part":
                            t, k = n
                            if k == 0:
                                pe.wait_ge(gate_done, layer * 3 * DK + i * 4 + (g0 + max(t - 1, 0) + START))
                                arrived(t0 + t, first + i * 4)
                            c = slice(k * P, k * P + P)
                            last = three(psum[:, 6 + t % 2, :], wh[:, (t0 + t) % WS, c], wl[:, (t0 + t) % WS, c],
                                         xh[:, k], xl[:, k], k == 0, k == DK - 1)
                            if k == DK - 1:
                                last.then_inc(tile_used, 1)
                            continue
                        hd, qt = n // NT, n % NT
                        w = width(qt)
                        if kind == "prep" and mixer == "B":
                            pe.wait_ge(staged, layer * 28 + i * 12 + 3 * (n + 1))
                            turn_blocks([stage_q[:, n % 2, b] for b in range(NT)], BQ)
                            turn_blocks([stage_k[:, n % 2, b] for b in range(NT)], BQ)
                            ready_at[n] = r
                        elif kind == "prep":
                            pe.wait_ge(staged, layer * 28 + i * 2 + (24 + n + 1))
                            turn_blocks([stage_a[:, n % 2, b] for b in range(NT)], P)
                            ready_at[n] = r
                        elif kind == "score":
                            pe.wait_ge(masked, unit + (max(n - 1, 0) + START))
                            if mixer == "B":
                                pe.wait_ge(turn_out, turn + (ready_at[hd] + START))
                                q, k = qt_buf[0:BQ, hd % 2, qt * P:qt * P + P], kt_buf[0:BQ, hd % 2, 0:w]
                            else:
                                rows = slice(AD * (hd % 2), AD * (hd % 2) + AD)
                                pe.wait_ge(turn_out, turn + (ready_at[hd // 2] + START))
                                q, k = qt_buf[rows, hd // 2, qt * P:qt * P + P], ka_t[rows, 0:w]
                            nc.tensor.matmul(psum[:, n % 2, 0:w], q, k, start=True, stop=True).then_inc(score_ready, 1)
                        elif kind == "turn":
                            pe.wait_ge(prob_ready, unit + (n + 1))
                            turn_blocks([pbuf[:, n % 2, b * P:b * P + P] for b in range(qt + 1)], P)
                            turn_at[n] = r
                        elif kind == "value":
                            pe.wait_ge(turn_out, turn + (turn_at[n] + START))
                            pe.wait_ge(value_out, unit + (max(n - 1, 0) + START))
                            for b in range(qt + 1):
                                if mixer == "B":
                                    v = ukv[:, b, bass.ds(i * (HEADS * P) + (hd * P + BN), BV)]
                                else:
                                    v = h_idx[:, b, G_VA:G_VA + AD]
                                last = nc.tensor.matmul(psum[:, 4 + n % 2, 0:BV], ptbuf[:, n % 2, b * P:b * P + P],
                                                        v, start=(b == 0), stop=(b == qt))
                            last.then_inc(value_ready, 1)
                        elif kind == "out":
                            pe.wait_ge(value_out, unit + (UNITS + START))
                            turn_blocks([ystage[:, b, n * P:n * P + P] for b in range(NT)], P)
                    assert r == per_body

            def norm(layer, n, after_mean):
                x0 = layer * 16 + 8 * n
                for j in range(DK):
                    pe.wait_ge(u_ready, x0 + (j + 1 + 2))
                    last = nc.tensor.matmul(psum[:, 0, :], ones_d[:], u[:, j], start=(j == 0), stop=(j == DK - 1))
                last.then_inc(mean_ready, 1)
                after_mean()
                for j in range(DK):
                    pe.wait_ge(squared, x0 + (j + 1))
                    nc.tensor.matmul(psum[:, 1, :], ones_d[:], sq[:, j % 2], start=(j == 0),
                                     stop=(j == DK - 1)).then_inc(var_step, 1)

            def embedding(q, layer, first):
                if q == 1:
                    pe.wait_ge(pp_out, layer * DK + 4)
                project(T_PP + q, first, ph, pl, 2, [2, 3, 4, 5])

            def down(t, first, k, start, stop):
                arrived(t, first)
                for j in range(DK):
                    c = slice(j * P, j * P + P)
                    last = three(psum[:, j, :], wh[:, t % WS, c], wl[:, t % WS, c], hh[:, k, :], hl[:, k, :],
                                 start, stop)
                    if stop and j < DK - 1:
                        last.then_inc(ffn_out, 1)
                last.then_inc(tile_used, 1)

            for s in (tile_used, turned, score_ready, value_ready):
                pe.sem_inc(s, START)
            pe.wait_ge(consts_ready, 5)
            pe.sem_inc(passed, 1)
            with pe.Fori(0, L) as layer:
                first = layer * TILES
                for kind, n in FRONT:
                    if kind == "scratch":
                        scratch(n, layer)
                    elif n in tile_group:
                        group(n, layer, first)
                    else:
                        j, value = (n - T_CONV) // 2, (n - T_CONV) % 2
                        if n == T_CONV:
                            pe.wait_ge(group_out, layer * 40 + 16)
                        if j >= 1:
                            pe.wait_ge(conv_in if value else conv_th, layer * CK + j)
                        project(n, first, xh, xl, DK, [6 + value])
                pe.wait_ge(group_out, layer * 40 + 40)
                pe.sem_inc(passed, 1)
                attention("B", layer, first)
                attention("A", layer, first)

                pe.wait_ge(conv_done, layer * CK + CK)
                pe.wait_ge(masked, layer * PAIRS + (PAIRS + START))
                for j in range(CK):
                    last = nc.tensor.matmul(psum[:, 0, :], ones_c[:], conv[:, j], start=(j == 0), stop=(j == CK - 1))
                last.then_inc(stat_ready, 1)
                for k in range(DK):
                    if k == 4:
                        for j in range(CK):
                            pe.wait_ge(squared_c, layer * CK + (j + 1))
                            last = nc.tensor.matmul(psum[:, 1, :], ones_c[:], csq[:, j], start=(j == 0),
                                                    stop=(j == CK - 1))
                        last.then_inc(stat_ready, 1)
                    pe.wait_ge(gate_done, layer * 3 * DK + (2 * DK + k - 1 + START))
                    project(T_GC + k, first, xh, xl, DK, [6 + k % 2])
                for q in range(12):
                    pair, br = q // 3, q % 3
                    if q == 0:
                        pe.wait_ge(gate_done, layer * 3 * DK + (3 * DK + START))
                        pe.wait_ge(value_out, layer * PAIRS + (PAIRS + START))
                        pe.wait_ge(y_low, layer * 6 + 2)
                    if q == 2:
                        pe.wait_ge(y_low, layer * 6 + 6)
                    if q >= 2:
                        pe.wait_ge(branch_out, layer * 24 + 2 * (q - 1))
                    project(T_BR + q, first, yh[br], yl[br], 4, [4 + 2 * (q % 2), 5 + 2 * (q % 2)])
                pe.wait_ge(merged_low, layer * DK + DK)
                pe.wait_ge(branch_out, layer * 24 + 24)
                pe.sem_inc(passed, 1)
                with pe.Fori(0, 2) as i:
                    for k in range(4):
                        pe.wait_ge(u_ready, layer * 16 + i * 4 + (k + 1))
                        project(T_OUT + k, first + i * 4, mh, ml, DK, [6 + k % 2])

                def first_embedding():
                    pe.wait_ge(p_low, layer + 1)
                    embedding(0, layer, first)

                norm(layer, 0, first_embedding)
                embedding(1, layer, first)
                with pe.Fori(0, 2) as i:
                    for k in range(4):
                        pe.wait_ge(ple_th, layer * DK + i * 4 + (k + 1))

                        def ready(kk):
                            pe.wait_ge(x_ready, layer * 16 + (DK + kk + 1))

                        project(T_PG + k, first + i * 4, xh, xl, DK, [6 + k % 2], ready if k == 0 else None)
                pe.wait_ge(pp_out, layer * DK + DK)
                pe.wait_ge(ple_th, layer * DK + (DK + 2))
                pe.sem_inc(passed, 1)
                with pe.Fori(0, FK // 2) as i:
                    for c in range(2):
                        pe.wait_ge(h_done, layer * (DK + FK) + i * 2 + (DK + c + 1))
                        project(T_FI + 2 * c, first + i * 4, xh, xl, DK, [4 + 2 * c])
                        project(T_FI + 2 * c + 1, first + i * 4, xh, xl, DK, [5 + 2 * c])
                pe.wait_ge(h_done, layer * (DK + FK) + (DK + FK + 2))
                down(T_FO, first, 0, True, False)
                with pe.Fori(0, (FK - 2) // 4) as i:
                    for k in range(4):
                        arrived(T_FO + 1 + k, first + i * 4)
                        kk = bass.ds(i * 4 + (1 + k), 1)
                        s = (T_FO + 1 + k) % WS
                        for j in range(DK):
                            c = slice(j * P, j * P + P)
                            xh_ = hh[:, kk, :].rearrange("p a n -> p (a n)")
                            xl_ = hl[:, kk, :].rearrange("p a n -> p (a n)")
                            last = three(psum[:, j, :], wh[:, s, c], wl[:, s, c], xh_, xl_, False, False)
                        last.then_inc(tile_used, 1)
                down(TILES - 1, first, FK - 1, False, True)
                norm(layer, 1, lambda: None)

        @block.vector
        def _(dve):
            v = nc.vector
            steps = Steps(dve, vec)

            def rope(x, heads, half, c0, dst, done, count):
                x1, x2 = x[:, :, :, 0:half], x[:, :, :, half:2 * half]
                c = cos[:, :, c0:c0 + half].unsqueeze(2).to_broadcast([P, NT, heads, half])
                s = sin[:, :, c0:c0 + half].unsqueeze(2).to_broadcast([P, NT, heads, half])
                n = NT * heads * half
                t1, t2, t3 = [rope_tmp[:, k, 0:n].rearrange("p (t h d) -> p t h d", t=NT, h=heads) for k in range(3)]
                steps.done(v.tensor_tensor(t1, x1, c, ALU.mult))
                steps.done(v.tensor_tensor(t2, x2, s, ALU.mult))
                steps.done(v.tensor_tensor(t3, x1, s, ALU.mult))
                steps.done(v.tensor_tensor(x2, x2, c, ALU.mult))
                steps.wait()
                steps.done(v.tensor_tensor(dst[:, :, :, 0:half], t1, t2, ALU.subtract))
                v.tensor_tensor(dst[:, :, :, half:2 * half], x2, t3, ALU.add).then_inc(done, 1)
                steps.wait()
                dve.wait_ge(done, count)

            dve.sem_inc(u_ready, 2)
            dve.sem_inc(h_done, 2)
            for s in (masked, value_out):
                dve.sem_inc(s, START)
            dve.wait_ge(tables_in, 32)
            ang = rope_tmp[:, 0, 64:256].rearrange("p (t f) -> p t f", t=NT)
            red = rope_tmp[:, 1, 0:192].rearrange("p (t f) -> p t f", t=NT)
            turns = rope_tmp[:, 1, 192:384].rearrange("p (t f) -> p t f", t=NT)
            quarter = rope_tmp[:, 2, 0:192].rearrange("p (t f) -> p t f", t=NT)
            pi = float(np.float32(3.1415925))
            two_pi = [6.28125, float(np.float32(2 * np.pi - 6.28125))]
            two_pi.append(float(2 * np.pi - 6.28125 - two_pi[1]))
            magic = 12582912.0
            two_pi[1] = float(np.float32(round(two_pi[1] * 2 ** 20) / 2 ** 20))
            two_pi[2] = float(2 * np.pi - 6.28125 - two_pi[1])
            steps.stage(0)
            setup = Steps(dve, angle_step)
            setup.done(v.tensor_copy(posf, posi))
            setup.wait()
            for b in range(NT):
                setup.done(v.tensor_scalar(ang[:, b], rope_tmp[:, 0, 0:48], posf[:, b:b + 1], None, ALU.mult))
            setup.wait()
            setup.done(v.tensor_scalar(turns, ang, float(1 / (2 * np.pi)), magic, ALU.mult, ALU.add))
            setup.wait()
            setup.done(v.tensor_scalar(turns, turns, magic, None, ALU.subtract))
            setup.wait()
            src = ang
            for c in two_pi:
                setup.done(v.scalar_tensor_tensor(red, turns, -c, src, ALU.mult, ALU.add))
                setup.wait()
                src = red
            setup.done(v.tensor_scalar(red, red, pi, -pi, ALU.min, ALU.max))
            setup.wait()
            setup.done(v.scalar_tensor_tensor(quarter, red, -1.0, red, ALU.mult, ALU.max))
            setup.wait()
            v.tensor_copy(posf, posf).then_inc(angles, 1)
            v.tensor_scalar(quarter, quarter, -1.0, float(np.pi / 2), ALU.mult, ALU.add).then_inc(angles, 1)
            for j in range(DK):
                dve.wait_ge(x_high, j + 1)
                v.tensor_tensor(xl[:, j], u[:, j], xh[:, j].bitcast(F32), ALU.subtract).then_inc(x_ready, 1)
            dve.wait_ge(tables, 2)
            dve.wait_ge(consts_ready, 5)

            def attention(mixer, layer, base, n_steps):
                steps_, per_body = (STEPS_B, TURNS_B) if mixer == "B" else (STEPS_A, TURNS_A)
                u0, r0, chunk0 = (0, 0, 0) if mixer == "B" else (BH * NT, 2 * TURNS_B, 2)
                scale = BQ ** -0.5 if mixer == "B" else AD ** -0.5
                turn_at, r = {}, 0
                for kind, n in steps_:
                    if kind == "prep":
                        r += 2 if mixer == "B" else 1
                    elif kind in ("turn", "out"):
                        r += 1
                        if kind == "turn":
                            turn_at[n] = r
                with dve.Fori(0, 2) as i:
                    unit = layer * PAIRS + i * UNITS + u0
                    turn = layer * TURNS + i * per_body + r0
                    steps.stage(layer * V_LAYER + i * n_steps + base)

                    def mask(n):
                        qt = n % NT
                        w = width(qt)
                        bias = causal[:, S - w:S] if mixer == "B" or qt == 0 else keep_bias[:, wide(qt):wide(qt) + w]
                        dve.wait_ge(score_ready, unit + (n + 1 + START))
                        dve.wait_ge(turned, turn + ((turn_at[n - 2] if n >= 2 else 0) + START))
                        dve.sem_inc(passed, 1)
                        v.tensor_tensor_reduce(pbuf[:, n % 2, 0:w], psum[:, n % 2, 0:w], bias, -scale, 3e38, ALU.add,
                                               ALU.min, nmax[:, n % 2:n % 2 + 1]).then_inc(masked, 1)

                    def normalise(n):
                        hd, qt = n // NT, n % NT
                        dve.wait_ge(value_ready, unit + (n + 1 + START))
                        if n == 0:
                            dve.wait_ge(turned, turn + START)
                        steps.done(v.reciprocal(rinv[:, n % 2:n % 2 + 1], psums[:, n % 4:n % 4 + 1]))
                        steps.wait()
                        v.tensor_scalar(ystage[:, qt, hd * AD:hd * AD + AD], psum[:, 4 + n % 2, 0:AD],
                                        rinv[:, n % 2:n % 2 + 1], None, ALU.mult).then_inc(value_out, 1)

                    def tap(k):
                        j = i + chunk0
                        h = hconv[:, bass.ds(j, 1), k:k + S].rearrange("p a n -> p (a n)")
                        acc = conv[:, bass.ds(j, 1), :].rearrange("p a n -> p (a n)")
                        w = par[:, bass.ds(i * CW + (PAR["cw"] + chunk0 * CW + k), 1)]
                        if k == 0:
                            b = par[:, bass.ds(i + (PAR["cb"] + chunk0), 1)]
                            steps.done(v.tensor_scalar(acc, h, w, b, ALU.mult, ALU.add))
                        else:
                            steps.wait()
                            ins = v.scalar_tensor_tensor(acc, h, w, acc, ALU.mult, ALU.add)
                            if k < CW - 1:
                                steps.done(ins)
                            else:
                                ins.then_inc(conv_done, 1)

                    for n in range(UNITS):
                        mask(n)
                        if n >= 2:
                            normalise(n - 2)
                        for k in range(2 * n, min(2 * n + 2, CW)):
                            tap(k)
                    normalise(UNITS - 2)
                    normalise(UNITS - 1)
                steps.end("V_ATTN_" + mixer, n_steps)

            def norm(layer, n, base, g, b):
                x0 = layer * 16 + 8 * n
                steps.stage(layer * V_LAYER + base)
                dve.wait_ge(mean_ready, layer * 2 + (n + 1))
                for j in range(DK):
                    v.tensor_tensor(u[:, j], u[:, j], psum[:, 0, :], ALU.subtract).then_inc(centered, 1)
                dve.wait_ge(sd_ready, layer * 2 + (n + 1))
                steps.done(v.reciprocal(rstd[:], rstd[:]))
                steps.wait()
                for j in range(DK + 1):
                    if j < DK:
                        steps.done(v.tensor_tensor(u[:, j], u[:, j], rstd[:], ALU.mult))
                    if j >= 1:
                        dve.wait_ge(x_high, x0 + (DK + j))
                        v.tensor_tensor(xl[:, j - 1], u[:, j - 1], xh[:, j - 1].bitcast(F32),
                                        ALU.subtract).then_inc(x_ready, 1)
                    if j < DK:
                        steps.wait()
                        v.tensor_scalar(u[:, j], u[:, j], column(g, j), column(b, j), ALU.mult,
                                        ALU.add).then_inc(z_ready, 1)
                steps.end("V_LN", V_LN)

            dve.sem_inc(passed, 1)
            with dve.Fori(0, L) as layer:
                first = layer * TILES
                steps.stage(layer * V_LAYER)
                dve.wait_ge(par_loaded, layer * 16 + 16)
                steps.done(v.tensor_scalar(par[:, 0:HALVED], par[:, 0:HALVED], 0.5, None, ALU.mult))
                dve.wait_ge(group_out, layer * 40 + 4)
                for k in range(2):
                    rope(h_idx[:, :, 192 * k:192 * k + 192].rearrange("p t (h d) -> p t h d", h=3), 3, AD // 2, 0,
                         h_idx[:, :, 192 * k:192 * k + 192].rearrange("p t (h d) -> p t h d", h=3), roped_idx,
                         layer * 2 + (k + 1))
                steps.done(v.tensor_scalar(wi_half, h_idx[:, :, G_WI:G_WI + IH], IH ** -0.5, None, ALU.mult))
                steps.done(v.memset(hconv[:, :, 0:CW - 1], 0.0))
                dve.wait_ge(group_out, layer * 40 + 8)
                rope(h_cq[:, :, QL:QL + BR].unsqueeze(2), 1, BR // 2, AD // 2, key_rope.unsqueeze(2), roped_u,
                     layer * 2 + 1)
                dve.wait_ge(ssq_ready, layer * 8 + (8 + START))
                v.tensor_scalar(rms[:, 0:4], ssq[:, 0:4], 1.0 / QL, RMS_EPS, ALU.mult, ALU.add).then_inc(var_rms, 1)
                v.tensor_scalar(rms[:, 4:8], ssq[:, 4:8], 1.0 / KVL, RMS_EPS, ALU.mult, ALU.add).then_inc(var_rms, 1)
                dve.wait_ge(sd_rms, layer + 1)
                steps.done(v.reciprocal(rms, rms))
                steps.wait()
                for b in range(NT):
                    v.tensor_scalar(h_cq[:, b, 0:QL], h_cq[:, b, 0:QL], rms[:, b:b + 1], None,
                                    ALU.mult).then_inc(normed_c, 1)
                for b in range(NT):
                    v.tensor_scalar(h_ckv[:, b, :], h_ckv[:, b, :], rms[:, 4 + b:5 + b], None,
                                    ALU.mult).then_inc(normed_c, 1)
                dve.wait_ge(group_out, layer * 40 + 16)
                for k in range(2):
                    x = h_qa[:, :, 256 * k:256 * k + 256].rearrange("p t (h d) -> p t h d", h=4)
                    rope(x, 4, AD // 2, 0, x, roped_q, layer * 2 + (k + 1))

                def c_lows(n):
                    dve.wait_ge(scratch_act, layer * SCRATCH + (n + 1))
                    v.scalar_tensor_tensor(cl[:, n - 4], psum[:, n % 4, :], column("gq", n - 4),
                                           ch[:, n - 4].bitcast(F32), ALU.mult, ALU.subtract).then_inc(c_low, 1)

                def conv_input(j):
                    dve.wait_ge(conv_th, layer * CK + (j + 1))
                    dve.wait_ge(tile_used, first + (T_CONV + 2 * j + 2 + START))
                    v.scalar_tensor_tensor(hconv[:, j, CW - 1:CW - 1 + S], th_conv[:, j % 2], 1.0, psum[:, 7, :],
                                           ALU.add, ALU.mult).then_inc(conv_in, 1)

                def block_scores(q):
                    for h in range(IH):
                        n = SCRATCH_T + IH * q + h
                        qt = logit(n)[0]
                        w, k = width(qt), IH * q + h
                        sc = scores[:, wide(qt):wide(qt) + w]
                        dve.wait_ge(scratch_act, layer * SCRATCH + (n + 1))
                        if h == 0:
                            v.tensor_scalar(sc, relu[:, k % 2, 0:w], wi_half[:, qt, 0:1], None,
                                            ALU.mult).then_inc(scored, 1)
                        else:
                            dve.wait_ge(scored, layer * 12 + k)
                            v.scalar_tensor_tensor(sc, relu[:, k % 2, 0:w], wi_half[:, qt, h:h + 1], sc, ALU.mult,
                                                   ALU.add).then_inc(scored, 1)
                    dve.wait_ge(scored, layer * 12 + (k + 1))
                    steps.done(v.tensor_tensor(sc[:, w - P:w], sc[:, w - P:w], causal[:, S - P:S], ALU.add))

                for n in range(4, SCRATCH_T):
                    c_lows(n)
                conv_input(0)
                block_scores(0)
                block_scores(1)
                conv_input(1)
                block_scores(2)
                steps.wait()
                for k in range(TOPK // 8):
                    for part in range(2):
                        for qt in range(NT - 1, 0, -1):
                            span = slice(wide(qt), wide(qt) + width(qt))
                            src = scores[:, span] if k == 0 else work[:, span]
                            best = top8[:, 8 * (qt - 1):8 * qt]
                            steps.wait(back=2)
                            dve.sem_inc(passed, 1)
                            if part == 0:
                                steps.done(v.max(best, src))
                            else:
                                steps.done(v.match_replace(work[:, span], best, src, TAKEN))
                    if k in (3, 8):
                        conv_input(2 if k == 3 else 3)
                steps.wait()
                steps.done(v.tensor_scalar(keep_bias[:], work[:], -2e38, NEG, ALU.is_gt, ALU.mult))
                dve.wait_ge(group_out, layer * 40 + 32)
                x = uq[:].rearrange("p t (h d) -> p t h d", h=BH)[:, :, :, BN:BQ]
                rope(x, BH, BR // 2, AD // 2, x, roped_u, layer * 2 + 2)
                steps.end("V_FRONT", V_FRONT)
                dve.sem_inc(passed, 1)
                attention("B", layer, VS_B, V_ATTN_B)
                attention("A", layer, VS_A, V_ATTN_A)

                steps.stage(layer * V_LAYER + VS_CONV)
                dve.wait_ge(y_high, layer * 6 + 1)
                v.tensor_tensor(yl[1][:], yb[:], yh[1][:].bitcast(F32), ALU.subtract).then_inc(y_low, 1)
                dve.wait_ge(y_high, layer * 6 + 2)
                v.tensor_tensor(yl[0][:], ya[:], yh[0][:].bitcast(F32), ALU.subtract).then_inc(y_low, 1)
                dve.wait_ge(stat_ready, layer * 2 + 1)
                for j in range(CK):
                    v.tensor_tensor(conv[:, j], conv[:, j], psum[:, 0, :], ALU.subtract).then_inc(centered_c, 1)
                dve.wait_ge(sd_c, layer + 1)
                steps.done(v.reciprocal(rstd_c[:], rstd_c[:]))
                steps.wait()
                for j in range(CK):
                    steps.done(v.tensor_tensor(conv[:, j], conv[:, j], rstd_c[:], ALU.mult))
                    steps.wait()
                    v.tensor_scalar(conv[:, j], conv[:, j], column("clg", j), column("clb", j), ALU.mult,
                                    ALU.add).then_inc(z_conv, 1)
                for j in range(CK + 1):
                    if j < CK:
                        dve.wait_ge(th_ready, layer * CK + (j + 1))
                        v.scalar_tensor_tensor(conv[:, j], th_z[j % 2][:], 1.0, conv[:, j], ALU.add,
                                               ALU.mult).then_inc(y2_ready, 1)
                    if j >= 1:
                        dve.wait_ge(y_high, layer * 6 + (2 + j))
                        v.scalar_tensor_tensor(yl[2][:, j - 1], conv[:, j - 1], 0.5, yh[2][:, j - 1].bitcast(F32),
                                               ALU.mult, ALU.subtract).then_inc(y_low, 1)
                steps.end("V_CONV", V_CONV)

                steps.stage(layer * V_LAYER + VS_BRANCH)
                for q in range(12):
                    pair, br = q // 3, q % 3
                    dve.wait_ge(tile_used, first + (T_BR + q + 1 + START))
                    if q == 0:
                        dve.wait_ge(gate_done, layer * 3 * DK + (3 * DK + START))
                    elif br == 0:
                        dve.wait_ge(merged_low, layer * DK + 2 * pair)
                    for c in range(2):
                        bank, g = psum[:, 4 + 2 * (q % 2) + c, :], (ga, gb, gc)[br][:, 2 * pair + c]
                        if br == 0:
                            v.scalar_tensor_tensor(msum[:, c], g, 1.0, bank, ALU.add, ALU.mult).then_inc(branch_out, 1)
                        else:
                            v.scalar_tensor_tensor(tmp[:], g, 1.0, bank, ALU.add, ALU.mult).then_inc(branch_out, 1)
                            dve.wait_ge(branch_out, layer * 24 + (2 * q + c + 1))
                            ins = v.tensor_tensor(msum[:, c], msum[:, c], tmp[:], ALU.add)
                            if br == 1:
                                steps.done(ins)
                                steps.wait()
                            else:
                                ins.then_inc(merged, 1)
                                dve.wait_ge(merged, layer * DK + (2 * pair + c + 1))
                    if br == 2:
                        for c in range(2):
                            n = 2 * pair + c
                            dve.wait_ge(merged_high, layer * DK + (n + 1))
                            v.scalar_tensor_tensor(ml[:, n], msum[:, c], 0.5, mh[:, n].bitcast(F32), ALU.mult,
                                                   ALU.subtract).then_inc(merged_low, 1)
                steps.end("V_BRANCH", V_BRANCH)
                dve.wait_ge(p_high, layer + 1)
                v.tensor_tensor(pl[:], praw[:], ph[:].bitcast(F32), ALU.subtract).then_inc(p_low, 1)

                dve.wait_ge(out_stored, layer * 16 + 16 * START)
                dve.sem_inc(passed, 1)
                with dve.Fori(0, 2) as i:
                    steps.stage(layer * V_LAYER + i * V_OUT + VS_OUT)
                    for k in range(4):
                        j = bass.ds(i * 4 + k, 1)
                        uj, xhj, xlj = [a[:, j, :].rearrange("p a n -> p (a n)") for a in (u, xh, xl)]
                        dve.wait_ge(tile_used, first + i * 4 + (T_OUT + k + 1 + START))
                        steps.done(v.scalar_tensor_tensor(uj, xhj.bitcast(F32), ALPHA, psum[:, 6 + k % 2, :], ALU.mult,
                                                          ALU.add))
                        steps.wait()
                        v.scalar_tensor_tensor(uj, xlj.bitcast(F32), ALPHA, uj, ALU.mult, ALU.add).then_inc(u_ready, 1)
                steps.end("V_OUT", V_OUT)
                norm(layer, 0, VS_LN1, "l1g", "l1b")

                dve.wait_ge(pp_out, layer * DK + DK)
                dve.sem_inc(passed, 1)
                with dve.Fori(0, 2) as i:
                    steps.stage(layer * V_LAYER + i * V_PG + VS_PG)
                    for k in range(4):
                        j = bass.ds(i * 4 + k, 1)
                        uj, ppj, xhj, xlj = [a[:, j, :].rearrange("p a n -> p (a n)") for a in (u, pp, xh, xl)]
                        dve.wait_ge(ple_th, layer * DK + i * 4 + (k + 1 + 2))
                        steps.done(v.scalar_tensor_tensor(uj, th[:, k % 2, :], 1.0, ppj, ALU.add, ALU.mult))
                        steps.wait()
                        steps.done(v.scalar_tensor_tensor(uj, xhj.bitcast(F32), ALPHA, uj, ALU.mult, ALU.add))
                        steps.wait()
                        v.scalar_tensor_tensor(uj, xlj.bitcast(F32), ALPHA, uj, ALU.mult, ALU.add).then_inc(h_done, 1)
                steps.end("V_PG", V_PG)

                with dve.Fori(0, FK // 2) as i:
                    steps.stage(layer * V_LAYER + i * V_FI + VS_FI)
                    for c in range(2):
                        tc = th[:, c, :]
                        dve.wait_ge(ffn_th, layer * FK + i * 2 + (c + 1))
                        steps.done(v.scalar_tensor_tensor(tc, tc, 1.0, psum[:, 4 + 2 * c, :], ALU.add, ALU.mult))
                        steps.wait()
                        dve.wait_ge(tile_used, first + i * 4 + (T_FI + 2 * c + 2 + START))
                        v.tensor_tensor(tc, tc, psum[:, 5 + 2 * c, :], ALU.mult).then_inc(ffn_s, 1)
                        dve.wait_ge(ffn_high, layer * FK + i * 2 + (c + 1))
                        hhj, hlj = [a[:, bass.ds(i * 2 + c, 1), :].rearrange("p a n -> p (a n)") for a in (hh, hl)]
                        v.scalar_tensor_tensor(hlj, tc, 0.5, hhj.bitcast(F32), ALU.mult,
                                               ALU.subtract).then_inc(h_done, 1)
                steps.end("V_FI", V_FI)
                for j in range(DK):
                    if j < DK - 1:
                        dve.wait_ge(ffn_out, layer * (DK - 1) + (j + 1))
                    else:
                        dve.wait_ge(tile_used, first + (TILES + START))
                    v.tensor_tensor(u[:, j], u[:, j], psum[:, j, :], ALU.add).then_inc(u_ready, 1)
                norm(layer, 1, VS_LN2, "l2g", "l2b")


def token_tiles(w, ncol, nk):
    k = w.shape[0] // P
    a = w.reshape(k // nk, nk, P, ncol).transpose(0, 2, 1, 3).reshape(k // nk, P, nk * ncol)
    return np.concatenate([a, np.zeros((k // nk, P, TILE - nk * ncol), w.dtype)], axis=2)


def feature_tiles(w, ncol):
    k = w.shape[0] // P
    return w.reshape(k, P, -1, ncol).transpose(2, 1, 0, 3).reshape(-1, P, k * ncol)


def weight_tiles(w_in, w_uq, w_ukv, w_branch, w_out, w_ffn_in, w_ffn_out, w_ple_gate, w_ple_proj):
    def cols(a, b):
        return w_in[:, a:b]

    idx = np.concatenate([cols(C_QI, C_WI), cols(C_KA, C_QI), cols(C_WI, C_CQ)], axis=1)
    cq = np.concatenate([cols(C_CQ, C_CKV), cols(C_KR, C_CA)], axis=1)
    tiles = [token_tiles(idx, 452, 2), token_tiles(cq, 416, 2), token_tiles(cols(C_CKV, C_KR), 256, 4),
             token_tiles(cols(C_QA, C_KA), 512, 2)]
    a, g = feature_tiles(cols(C_CA, C_CG), P), feature_tiles(cols(C_CG, C_GATE), P)
    for j in range(CK):
        tiles += [g[j:j + 1], a[j:j + 1]]
    tiles += [token_tiles(w_uq[:, 192 * g:192 * g + 192], 192, 3) for g in range(4)]
    tiles += [token_tiles(w_ukv[:, 512 * g:512 * g + 512], 512, 2) for g in range(2)]
    gates = feature_tiles(cols(C_GATE, N_IN), P)
    tiles.append(gates)
    br = [feature_tiles(w_branch[b], 2 * P) for b in range(3)]
    for j in range(4):
        tiles += [br[b][j:j + 1] for b in range(3)]
    tiles.append(feature_tiles(w_out, P))
    tiles.append(feature_tiles(w_ple_proj, 4 * P))
    tiles.append(feature_tiles(w_ple_gate, P))
    fi = feature_tiles(w_ffn_in, P)
    for j in range(FK):
        tiles += [fi[j:j + 1], fi[FK + j:FK + j + 1]]
    tiles.append(w_ffn_out.reshape(FK, P, D))
    return np.concatenate(tiles, axis=0)


_OUT = (L, P, DK, S)


def kernel(x, p, positions, w_in, b_gate, q_norm_g, w_uq, kv_norm_g, w_ukv, conv_w, conv_b, conv_ln_g, conv_ln_b,
           w_branch, w_out, ln1_g, ln1_b, w_ffn_in, w_ffn_out, w_ple_gate, w_ple_proj, ln2_g, ln2_b):
    import concourse.bacc as bacc
    from concourse.bass_utils import run_bass_kernel_spmd

    def arr(a):
        return np.ascontiguousarray(np.asarray(a))

    def columns(a):
        return arr(a).reshape(-1, P).T

    x, p, positions = arr(x), arr(p), arr(positions)
    ws = [arr(a) for a in (w_in, w_uq, w_ukv, w_branch, w_out, w_ffn_in, w_ffn_out, w_ple_gate, w_ple_proj)]
    tiles = np.concatenate([weight_tiles(*[w[i] for w in ws]) for i in range(L)], axis=0)
    params = []
    for i in range(L):
        taps = arr(conv_w)[i].T.reshape(CK, P, CW).transpose(1, 0, 2).reshape(P, CK * CW)
        params.append(np.concatenate(
            [columns(arr(b_gate)[i]), taps, columns(arr(q_norm_g)[i]), columns(arr(kv_norm_g)[i]),
             columns(arr(conv_b)[i]), columns(arr(conv_ln_g)[i]), columns(arr(conv_ln_b)[i]), columns(arr(ln1_g)[i]),
             columns(arr(ln1_b)[i]), columns(arr(ln2_g)[i]), columns(arr(ln2_b)[i])], axis=1))
    freq = [np.float32(1.0) / np.float32(THETA) ** (np.arange(0, n, 2, dtype=np.float32) / np.float32(n))
            for n in (AD, BR)]
    arrays = {
        "in_x": arr(x[0].T.reshape(DK, P, S).transpose(1, 0, 2)),
        "in_ple": arr(p[:, 0].transpose(0, 2, 1).reshape(L, PLE // P, P, S).transpose(0, 2, 1, 3)),
        "in_pos": arr(positions.reshape(NT, P).T),
        "in_freq": arr(np.broadcast_to(np.concatenate(freq).astype(np.float32), (P, 48))),
        "in_weights": arr(tiles),
        "in_params": arr(np.stack(params)),
    }
    nc = bacc.Bacc("TRN2", target_bir_lowering=False, num_devices=1)
    args = [nc.dram_tensor(n, a.shape, mybir.dt.from_np(a.dtype), kind="ExternalInput").ap()
            for n, a in arrays.items()]
    args.append(nc.dram_tensor("out", _OUT, F32, kind="ExternalOutput").ap())
    x_t, ple_t, pos, freq_t, weights, par, out = args
    build(nc, x_t, ple_t, pos, freq_t, weights, par, out)
    got = run_bass_kernel_spmd(nc, [arrays], core_ids=[0]).results[0]["out"]
    return arr(got[L - 1].transpose(2, 1, 0).reshape(1, S, D))
```

```python
from contextlib import ExitStack

import numpy as np

import concourse.bass as bass
from concourse import mybir

ALU = mybir.AluOpType
ACT = mybir.ActivationFunctionType
F32 = mybir.dt.float32
F32R = mybir.dt.float32r
I32 = mybir.dt.int32

P = 128
D = 1024
S = 512
L = 2
NT = S // P
DK = D // P
PLE = 256
AH, AD = 8, 64
IH, ID = 4, 64
TOPK = min(256, S // 4)
BH, BN, BR, BV = 8, 64, 32, 64
BQ = BN + BR
QL, KVL = 384, 256
CC, CW = 512, 31
CK = CC // P
FF = (8 * D + 3 * 256 - 1) // (3 * 256) * 256
FK = FF // P
THETA = 10000.0
LN_EPS, RMS_EPS = 1e-5, 1e-6
ALPHA = float((2 * L) ** 0.25)
assert TOPK == P

C_QA = 0
C_KA = C_QA + AH * AD
C_VA = C_KA + AD
C_QI = C_VA + AD
C_KI = C_QI + IH * ID
C_WI = C_KI + ID
C_CQ = C_WI + IH
C_CKV = C_CQ + QL
C_KR = C_CKV + KVL
C_CA = C_KR + BR
C_CG = C_CA + CC
C_GATE = C_CG + CC
N_IN = C_GATE + 3 * D

NEG = -1e30
TAKEN = -3e38

TOKEN_GROUPS = [("idx", 452, 2, 4), ("cq", 416, 2, 4), ("ckv", 256, 4, 2), ("qa", 512, 2, 4)]
TOKEN_GROUPS += [("uq", 192, 3, 1)] * 4 + [("ukv", 512, 2, 1)] * 2
G_KI, G_KA, G_VA, G_WI = 256, 320, 384, 448

T_CONV = 14
T_U = T_CONV + 4
T_GA = T_U + 6 + 4
T_GB = T_GA + DK
T_GC = T_GB + DK
T_BR = T_GC + DK
T_OUT = T_BR + 12
T_PP = T_OUT + DK
T_PG = T_PP + 4
T_FI = T_PG + DK
T_FO = T_FI + 2 * FK
PARTS = -(-FK // DK)
TILES = T_FO + PARTS * DK
assert TILES % 4 == 0
TILE = 1024
LEAD = 3
WS = 4
SPREAD = (2, 6)
CENTERED_DVE = 3
START = 1

PAR, _at = {}, 0
for _n, _c in (("bg", 3 * DK), ("cw", CK * CW), ("gq", 3), ("gkv", 2), ("cb", CK), ("clg", CK), ("clb", CK),
               ("l1g", DK), ("l1b", DK), ("l2g", DK), ("l2b", DK)):
    PAR[_n] = _at
    _at += _c
NPAR = _at
HALVED = PAR["gq"]

HEADS = 4
BEFORE_TURN, BEHIND_TURN = (0, 1, 1, 1), (1, 1, 1, 1)
UNITS = HEADS * NT


def attention_steps(prep_units):
    left = [(t, k) for t in range(4) for k in range(DK)]
    steps = []

    def parts(n):
        for _ in range(n):
            steps.append(("part", left.pop(0)))

    parts(1)
    steps.append(("prep", 0))
    parts(1)
    for s in range(UNITS):
        steps.append(("score", s))
        parts(BEFORE_TURN[s % NT])
        if s >= 1:
            steps.append(("turn", s - 1))
        parts(BEHIND_TURN[s % NT])
        if s >= 2:
            steps.append(("value", s - 2))
        if s % prep_units == 1 and s + prep_units < UNITS:
            steps.append(("prep", s // prep_units + 1))
    steps.append(("turn", UNITS - 1))
    steps.append(("value", UNITS - 2))
    steps.append(("value", UNITS - 1))
    parts(2)
    steps += [("out", 0), ("out", 1)]
    assert not left
    return steps


def scalar_steps(steps):
    order = []
    for kind, n in steps:
        if kind == "part":
            if n[1] == 0:
                order.append(("high", n[0]))
            elif n[1] == DK - 1:
                order.append(("gate", n[0]))
        elif kind == "turn" and ("score", n + 1) in order:
            order.insert(order.index(("score", n + 1)), (kind, n))
        else:
            order.append((kind, n))
    return order


STEPS_B = attention_steps(NT)
STEPS_A = attention_steps(2 * NT)
TURNS_B = 2 * HEADS + UNITS + 2
TURNS_A = HEADS // 2 + UNITS + 2
TURNS = 2 * (TURNS_B + TURNS_A)
PAIRS = AH * NT + BH * NT

SCRATCH_T = 9
SCRATCH = SCRATCH_T + IH * (NT - 1)
FRONT = [("tile", t) for t in range(T_CONV)] + [("scratch", n) for n in range(4)] + [("tile", T_CONV)]
FRONT += [("scratch", n) for n in range(4, SCRATCH_T)] + [("tile", T_CONV + 1)]
for _q in range(NT - 1):
    FRONT += [("scratch", SCRATCH_T + IH * _q + _h) for _h in range(IH)] + ([("tile", T_CONV + 2 + _q)] if _q < 2 else [])
FRONT += [("tile", t) for t in range(T_U, T_GA)]

CONV_PLACE = {}
for _j in range(CK):
    for _v in range(2):
        CONV_PLACE[(T_CONV if _j < 2 else T_U + 2) + 2 * _j + _v] = (_j, _v)

V_FRONT, V_ATTN_B, V_ATTN_A, V_CONV, V_BRANCH, V_LN1, V_LN2, V_PG, V_FI = 134, 46, 46, 5, 8, 31, 15, 8, 2
VS_B = V_FRONT
VS_A = VS_B + 2 * V_ATTN_B
VS_CONV = VS_A + 2 * V_ATTN_A
VS_BRANCH = VS_CONV + V_CONV
VS_LN1 = VS_BRANCH + V_BRANCH
VS_PG = VS_LN1 + V_LN1
VS_FI = VS_PG + 2 * V_PG
VS_LN2 = VS_FI + FK // 2 * V_FI
V_LAYER = VS_LN2 + V_LN2


class Steps:

    def __init__(self, engine, semaphore):
        self.engine, self.semaphore, self.base, self.n = engine, semaphore, 0, 0

    def stage(self, base):
        self.base, self.n = base, 0

    def done(self, instruction):
        instruction.then_inc(self.semaphore, 1)
        self.n += 1

    def wait(self, back=0):
        self.engine.wait_ge(self.semaphore, self.base + (self.n - back))

    def end(self, name, n):
        assert self.n == n, f"{name} has {self.n} steps"


def build(nc, x_t, ple_t, pos, freq, weights, params, out):
    with ExitStack() as ctx:
        BASE = 16512

        def sb(name, offset, shape, dt=F32):
            return nc.alloc_sbuf_tensor_at("sb_" + name, shape, dt, offset=BASE + offset)

        def sem(name):
            return ctx.enter_context(nc.semaphore(name))

        xh = sb("xh", 0, [P, DK, S], F32R)
        xl = sb("xl", 16384, [P, DK, S], F32R)
        wraw = sb("wraw", 32768, [P, 2, TILE])
        wh = sb("wh", 40960, [P, WS, TILE], F32R)
        wl = sb("wl", 57344, [P, WS, TILE], F32R)
        ident = sb("ident", 73728, [P, P])
        ones_d = sb("ones_d", 74240, [P, P])
        ones_c = sb("ones_c", 74752, [P, P])
        causal = sb("causal", 75264, [P, S])
        cos = sb("cos", 77312, [P, NT, 48])
        sin = sb("sin", 78080, [P, NT, 48])
        par = sb("par", 78848, [P, NPAR])
        praw = sb("praw", 79680, [P, 2, S])
        small = sb("small", 83776, [P, 256])
        A0 = 84800
        h_idx = sb("h_idx", A0 + 0, [P, NT, 452])
        h_qa = sb("h_qa", A0 + 7232, [P, NT, 512])
        h_cq = sb("h_cq", A0 + 15424, [P, NT, 416])
        h_ckv = sb("h_ckv", A0 + 22080, [P, NT, 256])
        conv = sb("conv", A0 + 17984, [P, CK, S])
        uq = sb("uq", A0 + 26176, [P, NT, BH * BQ])
        ukv = sb("ukv", A0 + 38464, [P, NT, BH * (BN + BV)])
        keep_bias = sb("keep_bias", A0 + 54848, [P, 1152])
        hconv = sb("hconv", A0 + 59456, [P, CK, CW - 1 + S])
        ga = sb("ga", A0 + 68128, [P, DK, S])
        ch = sb("ch", A0 + 68128, [P, 5, S], F32R)
        cl = sb("cl", A0 + 78368, [P, 5, S], F32R)
        yb = sb("yb", A0 + 84512, [P, 4, S])
        pbuf = sb("pbuf", A0 + 92704, [P, 2, S])
        ptbuf = sb("ptbuf", A0 + 96800, [P, 2, S])
        qt_buf = sb("qt_buf", A0 + 100896, [P, 2, S])
        kt_buf = sb("kt_buf", A0 + 104992, [P, 2, S])
        stage_q = sb("stage_q", A0 + 109088, [P, 2, NT, BQ])
        stage_k = sb("stage_k", A0 + 112160, [P, 2, NT, BQ])
        stage_a = sb("stage_a", A0 + 109088, [P, 2, NT, P])
        ystage = sb("ystage", A0 + 115232, [P, NT, HEADS * AD])
        work = sb("work", A0 + 92704, [P, 1152])
        scores = sb("scores", A0 + 119328, [P, 1152])
        qi_t = sb("qi_t", A0 + 101920, [P, 2, S])
        ki_t = sb("ki_t", A0 + 106016, [P, S])
        relu = sb("relu", A0 + 108064, [P, 2, S])
        th_conv = sb("th_conv", A0 + 88608, [P, 2, S])
        kdup = sb("kdup", A0 + 112160, [P, 2, NT, P])
        rope_tmp = sb("rope_tmp", A0 + 119328, [P, 3, 512])
        ka_t = sb("ka_t", A0 + 125472, [P, S])
        gb = sb("gb", A0 + 38464, [P, DK, S])
        ya = sb("ya", A0 + 26176, [P, 4, S])
        gc = sb("gc", A0 + 92704, [P, DK, S])
        csq = sb("csq", A0 + 109088, [P, CK, S])
        rstd_c = sb("rstd_c", A0 + 34368, [P, S])
        th_z = [sb("th_z0", A0 + 36416, [P, S]), sb("th_z1", A0 + 125472, [P, S])]
        tmp = sb("tmp", A0 + 36416, [P, S])
        yh = [sb("yah", A0 + 54848, [P, 4, S], F32R), sb("ybh", A0 + 0, [P, 4, S], F32R),
              sb("ych", A0 + 109088, [P, 4, S], F32R)]
        yl = [sb("yal", A0 + 117280, [P, 4, S], F32R), sb("ybl", A0 + 8192, [P, 4, S], F32R),
              sb("ycl", A0 + 84512, [P, 4, S], F32R)]
        msum = sb("msum", A0 + 63040, [P, 2, S])
        mh = sb("mh", A0 + 17984, [P, DK, S], F32R)
        ml = sb("ml", A0 + 68128, [P, DK, S], F32R)
        hh = sb("hh", A0 + 0, [P, FK, S], F32R)
        hl = sb("hl", A0 + 45056, [P, FK, S], F32R)
        u = sb("u", A0 + 90112, [P, DK, S])
        pp = sb("pp", A0 + 106496, [P, DK, S])
        th = sb("th", A0 + 122880, [P, 2, S])
        ph = sb("ph", A0 + 0, [P, 2, S], F32R)
        pl = sb("pl", A0 + 4096, [P, 2, S], F32R)
        sums = [sb("sums0", A0 + 34368, [P, 2, S]), sb("sums1", A0 + 106496, [P, 2, S])]
        sq = [sb("sq0", A0 + 38464, [P, 2, S]), sb("sq1", A0 + 110592, [P, 2, S])]
        ones_1 = sb("ones_1", A0 + 127520, [P, P])
        nmax = small[:, 0:2]
        psums = small[:, 2:6]
        rinv = small[:, 6:8]
        ssq = small[:, 8:16]
        rms = small[:, 16:24]
        eps_ln = small[:, 24:25]
        warm = small[:, 25:26]
        mean4, var4, scale4 = small[:, 76:80], small[:, 80:84], small[:, 84:88]
        posf = small[:, 26:30]
        wi_half = small[:, 32:48].rearrange("p (t h) -> p t h", t=NT)
        top8 = small[:, 48:72]
        posi = small[:, 72:76].bitcast(I32)
        key_rope = small[:, 128:256].rearrange("p (t r) -> p t r", t=NT)

        psum = ctx.enter_context(nc.psum_tensor("banks", [P, 8, 512], F32))

        raw_loaded = [sem("raw_loaded0"), sem("raw_loaded1")]
        hi_ready, lo_ready, tile_used = sem("hi_ready"), sem("lo_ready"), sem("tile_used")
        x_loaded = [sem(f"x_loaded{j}") for j in range(4)]
        consts_ready, zeroed, tables_in, angles, tables, angle_step = (
            sem("consts_ready"), sem("zeroed"), sem("tables_in"), sem("angles"), sem("tables"),
            sem("angle_step"))
        par_loaded, ple_loaded, out_stored = sem("par_loaded"), sem("ple_loaded"), sem("out_stored")
        group_out, roped_idx, dup_ready, ssq_ready, var_rms, sd_rms, normed_c = (
            sem("group_out"), sem("roped_idx"), sem("dup_ready"), sem("ssq_ready"), sem("var_rms"), sem("sd_rms"),
            sem("normed_c"))
        roped_q, roped_u = sem("roped_q"), sem("roped_u")
        scratch_ready, scratch_act, c_low, scored = (
            sem("scratch_ready"), sem("scratch_act"), sem("c_low"), sem("scored"))
        conv_th, conv_in = sem("conv_th"), sem("conv_in")
        staged, score_ready, masked, prob_ready, turned, turn_out, value_ready, value_out = (
            sem("staged"), sem("score_ready"), sem("masked"), sem("prob_ready"), sem("turned"), sem("turn_out"),
            sem("value_ready"), sem("value_out"))
        gate_done = sem("gate_done")
        conv_done, stat_ready, centered_c, squared_c, sd_c, z_conv, th_ready, y2_ready = (
            sem("conv_done"), sem("stat_ready"), sem("centered_c"), sem("squared_c"), sem("sd_c"), sem("z_conv"),
            sem("th_ready"), sem("y2_ready"))
        y_high, y_low, branch_out, merged, merged_high, merged_low = (
            sem("y_high"), sem("y_low"), sem("branch_out"), sem("merged"), sem("merged_high"), sem("merged_low"))
        u_ready, shift_sum, shift_ready, shifted, squared, sum_ready, sq_summed = (
            sem("u_ready"), sem("shift_sum"), sem("shift_ready"), sem("shifted"), sem("squared"), sem("sum_ready"),
            sem("sq_summed"))
        mean_ready, sq_ready, var_ready, warmed, sd_ready, diag_ready, spread, mean_copied = (
            sem("mean_ready"), sem("sq_ready"), sem("var_ready"), sem("warmed"), sem("sd_ready"), sem("diag_ready"),
            sem("spread"), sem("mean_copied"))
        centered, z_ready, x_high, x_ready, z_full = (
            sem("centered"), sem("z_ready"), sem("x_high"), sem("x_ready"), sem("z_full"))
        p_high, p_low, pp_out, ple_th, h_done, ffn_th, ffn_s, ffn_high = (
            sem("p_high"), sem("p_low"), sem("pp_out"), sem("ple_th"), sem("h_done"), sem("ffn_th"), sem("ffn_s"),
            sem("ffn_high"))
        vec = sem("vec")
        passed = sem("passed")

        def width(qt):
            return (qt + 1) * P

        def wide(qt):
            return sum(width(q) for q in range(1, qt))

        def column(name, j):
            return par[:, PAR[name] + j:PAR[name] + j + 1]

        block = ctx.enter_context(nc.Block())

        @block.sync
        def _(sp):
            for t in range(2):
                sp.dma_start(wraw[:, t, :], weights[t]).then_inc(raw_loaded[t], 16)
            def load(t, tile):
                sp.wait_ge(lo_ready, tile - 1)
                sp.dma_start(wraw[:, t, :], weights[bass.ds(tile, 1)].rearrange("a p n -> (a p) n")).then_inc(
                    raw_loaded[t], 16)

            with sp.Fori(1, L * TILES // 2 + 1) as m:
                for t in range(2):
                    load(t, m * 2 + t)
            sp.wait_ge(lo_ready, L * TILES + 1)
            sp.dma_start(wraw[:, 0, :], weights[L * TILES + 2]).then_inc(raw_loaded[0], 16)

        @block.gpsimd
        def _(pool):
            nc.gpsimd.memset(ident[:], 0.0).then_inc(zeroed, 1)
            nc.gpsimd.memset(causal[:], 0.0).then_inc(zeroed, 1)
            nc.gpsimd.memset(ones_d[:], 1.0 / D).then_inc(consts_ready, 1)
            nc.gpsimd.memset(ones_c[:], 1.0 / CC).then_inc(consts_ready, 1)
            nc.gpsimd.memset(ones_1[:], 1.0).then_inc(consts_ready, 1)
            nc.gpsimd.memset(eps_ln, LN_EPS).then_inc(consts_ready, 1)
            pool.wait_ge(zeroed, 2)
            nc.gpsimd.affine_select(out=ident[:], in_=ident[:], compare_op=ALU.not_equal, fill=1.0, base=0,
                                    pattern=[[-1, P]], channel_multiplier=1).then_inc(consts_ready, 1)
            nc.gpsimd.affine_select(out=causal[:, S - P:S], in_=causal[:, S - P:S], compare_op=ALU.is_ge, fill=NEG,
                                    base=0, pattern=[[-1, P]], channel_multiplier=1).then_inc(consts_ready, 1)

            def low(t, first):
                pool.wait_ge(hi_ready, first + (t + 1))
                nc.gpsimd.tensor_tensor(wl[:, t % WS, :], wraw[:, t % 2, :], wh[:, t % WS, :].bitcast(F32),
                                        ALU.subtract).then_inc(lo_ready, 1)

            def stage(mixer, i, layer, h):
                if mixer == "B":
                    per, uses, first = HEADS, STEPS_B, 0
                else:
                    per, uses, first = HEADS // 2, STEPS_A, 2 * TURNS_B
                per_body = TURNS_B if mixer == "B" else TURNS_A
                seen, turns = 0, 0
                for kind, n in uses:
                    if h >= 2 and seen == h - 1:
                        break
                    if kind == "prep":
                        seen += 1
                        turns += 2 if mixer == "B" else 1
                    if kind in ("turn", "out"):
                        turns += 1
                need = turns if h >= 2 else 0
                pool.wait_ge(turned, layer * TURNS + first + i * per_body + (need + START))
                if mixer == "B":
                    q = uq[:, :, bass.ds(i * (HEADS * BQ) + h * BQ, BQ)]
                    k = ukv[:, :, bass.ds(i * (HEADS * P) + h * P, BN)]
                    nc.gpsimd.tensor_copy(stage_q[:, h % 2], q).then_inc(staged, 1)
                    nc.gpsimd.tensor_copy(stage_k[:, h % 2, :, 0:BN], k).then_inc(staged, 1)
                    nc.gpsimd.tensor_copy(stage_k[:, h % 2, :, BN:BQ], key_rope).then_inc(staged, 1)
                else:
                    q = h_qa[:, :, bass.ds(i * (HEADS * AD) + h * P, P)]
                    nc.gpsimd.tensor_copy(stage_a[:, h % 2], q).then_inc(staged, 1)

            def center(layer, n):
                pool.wait_ge(mean_copied, layer * 2 + (n + 1))
                for j in range(CENTERED_DVE, DK):
                    nc.gpsimd.tensor_tensor(u[:, j], u[:, j], sq[n][:, 0], ALU.subtract).then_inc(centered, 1)

            for t in range(LEAD):
                low(t, 0)
            pool.sem_inc(passed, 1)
            with pool.Fori(0, L) as layer:
                first = layer * TILES
                with pool.Fori(0, T_GA // 4) as i:
                    for k in range(4):
                        low(LEAD + k, first + i * 4)
                pool.wait_ge(roped_u, layer * 2 + 2)
                pool.wait_ge(group_out, layer * 40 + 40)
                pool.sem_inc(passed, 1)
                with pool.Fori(0, 2) as i:
                    stage("B", i, layer, 0)
                    stage("B", i, layer, 1)
                    for k in range(4):
                        low(T_GA + LEAD + k, first + i * 4)
                        if k < HEADS - 2:
                            stage("B", i, layer, k + 2)
                pool.wait_ge(roped_q, layer * 2 + 2)
                pool.sem_inc(passed, 1)
                with pool.Fori(0, 2) as i:
                    stage("A", i, layer, 0)
                    stage("A", i, layer, 1)
                    for k in range(4):
                        low(T_GB + LEAD + k, first + i * 4)
                with pool.Fori(0, (T_PP - T_GC) // 4) as i:
                    for k in range(4):
                        low(T_GC + LEAD + k, first + i * 4)
                center(layer, 0)
                with pool.Fori(0, (TILES - T_PP) // 4) as i:
                    for k in range(4):
                        low(T_PP + LEAD + k, first + i * 4)
                center(layer, 1)

        def logit(n):
            k = n - SCRATCH_T
            return NT - 1 - k // IH, k % IH

        tile_group, t, col = {}, 0, {}
        for g, (name, ncol, nk, tiles) in enumerate(TOKEN_GROUPS):
            col[g] = sum(n for gg, (nm, n, _, _) in enumerate(TOKEN_GROUPS) if gg < g and nm == name)
            for k in range(tiles):
                tile_group[t] = (g, k)
                t += 1
            if t == T_CONV:
                t = T_U
        group_dst = {"idx": h_idx, "cq": h_cq, "ckv": h_ckv, "qa": h_qa, "uq": uq, "ukv": ukv}

        @block.scalar
        def _(act):
            act.dma_start(posi, pos).then_inc(tables_in, 16)
            act.dma_start(rope_tmp[:, 0, 0:48], freq).then_inc(tables_in, 16)
            for j in range(4):
                act.dma_start(u[:, 2 * j:2 * j + 2], x_t[:, 2 * j:2 * j + 2]).then_inc(x_loaded[j], 16)
            act.sem_inc(ple_th, 2)
            for s in (gate_done, turn_out, ssq_ready, warmed):
                act.sem_inc(s, START)
            act.wait_ge(angles, 2)
            nc.scalar.activation(sin[:], rope_tmp[:, 1, 0:192], ACT.Sin).then_inc(tables, 1)
            nc.scalar.activation(cos[:], rope_tmp[:, 2, 0:192], ACT.Sin).then_inc(tables, 1)
            for j in range(DK):
                if j % 2 == 0:
                    act.wait_ge(x_loaded[j // 2], 16)
                nc.scalar.activation(xh[:, j], u[:, j], ACT.Copy).then_inc(x_high, 1)
            act.wait_ge(consts_ready, 6)

            def high(t, first):
                act.wait_ge(tile_used, first + (max(t - (WS - 1), 0) + START))
                act.wait_ge(raw_loaded[t % 2], first * 8 + 16 * (t // 2 + 1))
                nc.scalar.activation(wh[:, t % WS, :], wraw[:, t % 2, :], ACT.Copy).then_inc(hi_ready, 1)

            def gate(t, first, bank, dst, bias, done):
                act.wait_ge(tile_used, first + (t + 1 + START))
                nc.scalar.activation(dst, psum[:, bank, :], ACT.Tanh, scale=0.5, bias=bias).then_inc(done, 1)

            def attention(mixer, layer, first):
                steps, per_body, t0 = (STEPS_B, TURNS_B, T_GA) if mixer == "B" else (STEPS_A, TURNS_A, T_GB)
                u0, r0 = (0, 0) if mixer == "B" else (BH * NT, 2 * TURNS_B)
                dst, y, g0 = (ga, yb, 0) if mixer == "B" else (gb, ya, DK)
                heads = 1 if mixer == "B" else 2
                order = scalar_steps(steps)
                with act.Fori(0, 2) as i:
                    unit = layer * PAIRS + i * UNITS + u0
                    turn = layer * TURNS + i * per_body + r0
                    r = 0

                    def turned_out(out, rows, w):
                        nonlocal r
                        act.wait_ge(turned, turn + (r + 1 + START))
                        nc.scalar.activation(out, psum[0:rows, 2 + r % 2, 0:w], ACT.Copy).then_inc(turn_out, 1)
                        r += 1

                    for kind, n in order:
                        if kind == "high":
                            high(t0 + n + LEAD, first + i * 4)
                        elif kind == "gate":
                            b = par[:, bass.ds(i * 4 + (PAR["bg"] + g0 + n), 1)]
                            o = dst[:, bass.ds(i * 4 + n, 1), :].rearrange("p a n -> p (a n)")
                            gate(t0 + n, first + i * 4, 6 + n % 2, o, b, gate_done)
                        elif kind == "prep":
                            act.wait_ge(score_ready, unit + (max(heads * NT * (n - 1), 0) + START))
                            if mixer == "B":
                                turned_out(qt_buf[0:BQ, n % 2, :], BQ, S)
                                turned_out(kt_buf[0:BQ, n % 2, :], BQ, S)
                            else:
                                turned_out(qt_buf[:, n % 2, :], P, S)
                        elif kind == "turn":
                            act.wait_ge(value_ready, unit + (max(n - 1, 0) + START))
                            turned_out(ptbuf[:, n % 2, 0:width(n % NT)], P, width(n % NT))
                        elif kind == "score":
                            w = width(n % NT)
                            act.wait_ge(masked, unit + (n + 1 + START))
                            nc.scalar.activation(pbuf[:, n % 2, 0:w], pbuf[:, n % 2, 0:w], ACT.Exp, scale=-1.0,
                                                 bias=nmax[:, n % 2:n % 2 + 1],
                                                 accum_out=psums[:, n % 4:n % 4 + 1]).then_inc(prob_ready, 1)
                        elif kind == "out":
                            turned_out(y[:, bass.ds(i * 2 + n, 1), :].rearrange("p a n -> p (a n)"), P, S)

            def squares(layer, n, j):
                x0 = layer * 16 + 8 * n
                if j < 4:
                    act.wait_ge(shifted, layer * 8 + (4 * n + j + 1))
                else:
                    act.wait_ge(u_ready, x0 + (j + 1 + 2))
                if j >= 3:
                    act.wait_ge(sq_summed, layer * 12 + (6 * n + j - 2))
                dst = sums[n][:, 1] if j == 0 else sq[n][:, j % 2]
                nc.scalar.activation(dst, u[:, j], ACT.Square).then_inc(squared, 1)

            def deviation(layer, n):
                act.wait_ge(warmed, layer * 2 + (n + START))
                nc.scalar.activation(warm, eps_ln, ACT.Sqrt).then_inc(warmed, 1)
                act.wait_ge(var_ready, layer * 2 + (n + 1))
                nc.scalar.activation(var4, var4, ACT.Sqrt, bias=eps_ln).then_inc(sd_ready, 1)
                act.wait_ge(spread, layer * 4 + (2 * n + 1))
                nc.scalar.activation(sq[n][:, 0], psum[:, SPREAD[n], :], ACT.Copy).then_inc(mean_copied, 1)

            def norm_high(layer, n, j):
                act.wait_ge(z_ready, layer * 16 + (8 * n + j + 1))
                nc.scalar.activation(xh[:, j], u[:, j], ACT.Identity,
                                     bias=column(("l1b", "l2b")[n], j)).then_inc(x_high, 1)

            for t in range(LEAD):
                high(t, 0)
            with act.Fori(0, L) as layer:
                first = layer * TILES
                for kind, n in FRONT:
                    if kind == "tile":
                        high(n + LEAD, first)
                        if n == 1:
                            act.wait_ge(x_ready, layer * 16 + DK)
                            act.dma_start(par[:], params[bass.ds(layer, 1)].rearrange("a p n -> (a p) n")).then_inc(
                                par_loaded, 16)
                            act.dma_start(praw[:], ple_t[bass.ds(layer, 1)].rearrange("a p k n -> (a p) k n")).then_inc(
                                ple_loaded, 16)
                        if n in tile_group:
                            g, k = tile_group[n]
                            name, ncol, _, tiles = TOKEN_GROUPS[g]
                            if k == tiles - 1:
                                act.wait_ge(tile_used, first + (n + 1 + START))
                                for b in range(NT):
                                    nc.scalar.activation(group_dst[name][:, b, col[g]:col[g] + ncol],
                                                         psum[:, 4 * (g % 2) + b, 0:ncol],
                                                         ACT.Copy).then_inc(group_out, 1)
                        elif CONV_PLACE[n][1] == 0:
                            j = CONV_PLACE[n][0]
                            if j >= 2:
                                act.wait_ge(conv_in, layer * CK + (j - 1))
                            gate(n, first, 6 if j < 2 else 0, th_conv[:, j % 2, :], 0.0, conv_th)
                        if n == 5:
                            act.wait_ge(roped_idx, layer * 2 + 2)
                            for w, c in ((0, G_KI), (1, G_KA)):
                                src = h_idx[:, :, c:c + AD].unsqueeze(2).to_broadcast([P, NT, 2, AD])
                                nc.scalar.activation(kdup[:, w].rearrange("p t (r d) -> p t r d", r=2), src,
                                                     ACT.Copy).then_inc(dup_ready, 1)
                        if n in (7, 9):
                            src, c, nn = (h_cq, QL, 0) if n == 7 else (h_ckv, KVL, NT)
                            for b in range(NT):
                                act.wait_ge(group_out, layer * 40 + (8 if n == 7 else 12))
                                act.wait_ge(ssq_ready, layer * 8 + (nn + b + START))
                                nc.scalar.activation(relu[:, 0, 0:c], src[:, b, 0:c], ACT.Square,
                                                     accum_out=ssq[:, nn + b:nn + b + 1]).then_inc(ssq_ready, 1)
                        if n == 11:
                            act.wait_ge(var_rms, layer * 2 + 2)
                            nc.scalar.activation(rms, rms, ACT.Sqrt).then_inc(sd_rms, 1)
                    else:
                        bank = n % 4
                        act.wait_ge(scratch_ready, layer * SCRATCH + (n + 1))
                        if n < 4:
                            dst = (qi_t[:, 0], qi_t[:, 1], ki_t[:], ka_t[:])[n]
                            nc.scalar.activation(dst, psum[:, bank, :], ACT.Copy).then_inc(scratch_act, 1)
                        elif n < SCRATCH_T:
                            if n == 4:
                                act.wait_ge(par_loaded, layer * 16 + 16)
                            nc.scalar.activation(ch[:, n - 4], psum[:, bank, :], ACT.Copy,
                                                 scale=column("gq", n - 4)).then_inc(scratch_act, 1)
                        else:
                            k, w = n - SCRATCH_T, width(logit(n)[0])
                            if k >= 2:
                                act.wait_ge(scored, layer * 12 + (k - 1))
                            nc.scalar.activation(relu[:, k % 2, 0:w], psum[:, bank, 0:w], ACT.Relu,
                                                 scale=ID ** -0.5).then_inc(scratch_act, 1)
                attention("B", layer, first)
                attention("A", layer, first)

                act.wait_ge(turn_out, layer * TURNS + (TURNS + START))
                act.wait_ge(masked, layer * PAIRS + (PAIRS + START))
                act.wait_ge(conv_done, layer * CK + CK)
                nc.scalar.activation(yh[1][:], yb[:], ACT.Copy).then_inc(y_high, 1)
                nc.scalar.activation(yh[0][:], ya[:], ACT.Copy).then_inc(y_high, 1)
                for k in range(DK):
                    t = T_GC + k
                    high(t + LEAD, first)
                    gate(t, first, 6 + k % 2, gc[:, k], column("bg", 2 * DK + k), gate_done)
                    if k == 0:
                        for j in range(CK):
                            act.wait_ge(centered_c, layer * CK + (j + 1))
                            nc.scalar.activation(csq[:, j], conv[:, j], ACT.Square).then_inc(squared_c, 1)
                    if k == 5:
                        act.wait_ge(stat_ready, layer * 2 + 2)
                        nc.scalar.activation(rstd_c[:], psum[:, 1, :], ACT.Sqrt, bias=eps_ln).then_inc(sd_c, 1)
                for j in range(CK + 1):
                    if j < CK:
                        act.wait_ge(z_conv, layer * CK + (j + 1))
                        if j >= 2:
                            act.wait_ge(y2_ready, layer * CK + (j - 1))
                        nc.scalar.activation(th_z[j % 2][:], conv[:, j], ACT.Tanh, scale=0.5).then_inc(th_ready, 1)
                    if j >= 1:
                        act.wait_ge(y2_ready, layer * CK + j)
                        nc.scalar.activation(yh[2][:, j - 1], conv[:, j - 1], ACT.Copy, scale=0.5).then_inc(y_high, 1)
                for q in range(12):
                    high(T_BR + q + LEAD, first)
                    if q % 3 == 2:
                        for c in range(2):
                            n = 2 * (q // 3) + c
                            act.wait_ge(merged, layer * DK + (n + 1))
                            nc.scalar.activation(mh[:, n], msum[:, c], ACT.Copy, scale=0.5).then_inc(merged_high, 1)
                act.wait_ge(ple_loaded, layer * 16 + 16)
                act.wait_ge(tile_used, first + (T_OUT + START))
                nc.scalar.activation(ph[:], praw[:], ACT.Copy).then_inc(p_high, 1)
                for k in range(DK):
                    high(T_OUT + k + LEAD, first)
                    for j in range(4) if k == 4 else range(k - 1, k) if k > 4 else ():
                        squares(layer, 0, j)
                squares(layer, 0, DK - 1)
                deviation(layer, 0)
                high(T_PP + LEAD, first)

                def embedding_out(q):
                    act.wait_ge(tile_used, first + (T_PP + q + 1 + START))
                    for c in range(2):
                        nc.scalar.activation(pp[:, 2 * q + c], psum[:, 4 + 2 * (q % 2) + c, :], ACT.Copy,
                                             scale=0.5).then_inc(pp_out, 1)

                for j in range(DK):
                    norm_high(layer, 0, j)
                    if j % 2 == 0:
                        embedding_out(j // 2)
                        if j < 6:
                            high(T_PP + j // 2 + 1 + LEAD, first)
                with act.Fori(0, 2) as i:
                    for k in range(4):
                        high(T_PG + k + LEAD, first + i * 4)
                        act.wait_ge(h_done, layer * (DK + FK) + i * 4 + (k + 1))
                        gate(T_PG + k, first + i * 4, k % 2, th[:, k % 2, :], 0.0, ple_th)
                with act.Fori(0, FK // 2) as i:
                    for c in range(2):
                        high(T_FI + 2 * c + LEAD, first + i * 4)
                        act.wait_ge(h_done, layer * (DK + FK) + i * 2 + (DK + c + 1))
                        gate(T_FI + 2 * c, first + i * 4, 4 + 2 * c, th[:, c, :], 0.0, ffn_th)
                        high(T_FI + 2 * c + 1 + LEAD, first + i * 4)
                        act.wait_ge(ffn_s, layer * FK + i * 2 + (c + 1))
                        nc.scalar.activation(hh[:, bass.ds(i * 2 + c, 1), :].rearrange("p a n -> p (a n)"),
                                             th[:, c, :], ACT.Copy, scale=0.5).then_inc(ffn_high, 1)
                for k in range(PARTS * DK):
                    high(T_FO + k + LEAD, first)
                    j = k // PARTS
                    if k % PARTS == 0 and j >= 4:
                        for jj in range(4) if j == 4 else range(j - 1, j):
                            squares(layer, 1, jj)
                squares(layer, 1, DK - 1)
                deviation(layer, 1)
                for j in range(DK):
                    norm_high(layer, 1, j)
            for j in range(0, DK, 2):
                act.wait_ge(z_full, (L - 1) * DK + j + 2)
                act.dma_start(out[:, j:j + 2], u[:, j:j + 2]).then_inc(out_stored, 16)
            act.wait_ge(out_stored, 16 * 4)

        @block.tensor
        def _(pe):
            def three(out, wh_, wl_, xh_, xl_, start, stop):
                nc.tensor.matmul(out, wh_, xh_, start=start, stop=False)
                nc.tensor.matmul(out, wh_, xl_, start=False, stop=False)
                return nc.tensor.matmul(out, wl_, xh_, start=False, stop=stop)

            def arrived(t, first):
                pe.wait_ge(lo_ready, first + (t + 1))

            def project(t, first, src_h, src_l, nk, outs, ready=None):
                arrived(t, first)
                n = len(outs) * P
                h = wh[:, t % WS, 0:nk * n].rearrange("p (k n) -> p k n", k=nk)
                lw = wl[:, t % WS, 0:nk * n].rearrange("p (k n) -> p k n", k=nk)
                for c, bank in enumerate(outs):
                    for k in range(nk):
                        if ready is not None and c == 0:
                            ready(k)
                        last = three(psum[:, bank, :], h[:, k, c * P:c * P + P], lw[:, k, c * P:c * P + P],
                                     src_h[:, k], src_l[:, k], k == 0, k == nk - 1)
                last.then_inc(tile_used, 1)

            def group(t, layer, first):
                g, part = tile_group[t]
                name, ncol, nk, tiles = TOKEN_GROUPS[g]
                if part == 0:
                    if g >= 2:
                        pe.wait_ge(group_out, layer * 40 + 4 * (g - 1))
                    if g == 4:
                        pe.wait_ge(scratch_act, layer * SCRATCH + SCRATCH)
                        pe.wait_ge(c_low, layer * 5 + 5)
                    if g == 5:
                        pe.wait_ge(conv_in, layer * CK + 2)
                arrived(t, first)
                src_h, src_l, k0 = (xh, xl, 0) if g < 4 else (ch, cl, 0 if name == "uq" else 3)
                h = wh[:, t % WS, 0:nk * ncol].rearrange("p (k n) -> p k n", k=nk)
                lw = wl[:, t % WS, 0:nk * ncol].rearrange("p (k n) -> p k n", k=nk)
                for kk in range(nk):
                    k = nk * part + kk
                    if g == 0:
                        pe.wait_ge(x_ready, layer * 16 + (k + 1))
                    for b in range(NT):
                        o = psum[:, 4 * (g % 2) + b, 0:ncol]
                        th_, tl_ = src_h[:, k0 + k, b * P:b * P + P], src_l[:, k0 + k, b * P:b * P + P]
                        nc.tensor.matmul(o, th_, h[:, kk], start=(k == 0), stop=False)
                        nc.tensor.matmul(o, th_, lw[:, kk], start=False, stop=False)
                        last = nc.tensor.matmul(o, tl_, h[:, kk], start=False, stop=(k == nk * tiles - 1))
                last.then_inc(tile_used, 1)

            def scratch(n, layer):
                if n >= 4:
                    pe.wait_ge(scratch_act, layer * SCRATCH + (n - 3))
                if 4 <= n - 4 < SCRATCH_T:
                    pe.wait_ge(c_low, layer * 5 + (n - 7))
                if n == 0:
                    pe.wait_ge(group_out, layer * 40 + 12)
                    pe.wait_ge(roped_idx, layer * 2 + 2)
                if n == 2:
                    pe.wait_ge(dup_ready, layer * 2 + 2)
                if n == 4:
                    pe.wait_ge(normed_c, layer * 8 + 8)
                if n < SCRATCH_T:
                    for b in range(NT):
                        if n < 2:
                            src = h_idx[:, b, n * P:n * P + P]
                        elif n < 4:
                            src = kdup[:, n - 2, b]
                        elif n < 7:
                            src = h_cq[:, b, (n - 4) * P:(n - 4) * P + P]
                        else:
                            src = h_ckv[:, b, (n - 7) * P:(n - 7) * P + P]
                        last = nc.tensor.transpose(psum[:, n % 4, b * P:b * P + P], src, ident[:])
                else:
                    qt, h = logit(n)
                    rows = slice(ID * (h % 2), ID * (h % 2) + ID)
                    last = nc.tensor.matmul(psum[:, n % 4, 0:width(qt)], qi_t[rows, h // 2, qt * P:qt * P + P],
                                            ki_t[rows, 0:width(qt)], start=True, stop=True)
                last.then_inc(scratch_ready, 1)

            def attention(mixer, layer, first):
                steps, per_body, t0 = (STEPS_B, TURNS_B, T_GA) if mixer == "B" else (STEPS_A, TURNS_A, T_GB)
                u0, r0, g0 = (0, 0, 0) if mixer == "B" else (BH * NT, 2 * TURNS_B, DK)
                with pe.Fori(0, 2) as i:
                    unit = layer * PAIRS + i * UNITS + u0
                    turn = layer * TURNS + i * per_body + r0
                    r, ready_at, turn_at = 0, {}, {}

                    def turn_blocks(blocks, rows):
                        nonlocal r
                        pe.wait_ge(turn_out, turn + (max(r - 1, 0) + START))
                        for b, src in enumerate(blocks):
                            last = nc.tensor.transpose(psum[0:rows, 2 + r % 2, b * P:b * P + P], src, ident[:])
                        last.then_inc(turned, 1)
                        r += 1

                    for kind, n in steps:
                        if kind == "part":
                            t, k = n
                            if k == 0:
                                pe.wait_ge(gate_done, layer * 3 * DK + i * 4 + (g0 + max(t - 1, 0) + START))
                                arrived(t0 + t, first + i * 4)
                            c = slice(k * P, k * P + P)
                            last = three(psum[:, 6 + t % 2, :], wh[:, (t0 + t) % WS, c], wl[:, (t0 + t) % WS, c],
                                         xh[:, k], xl[:, k], k == 0, k == DK - 1)
                            if k == DK - 1:
                                last.then_inc(tile_used, 1)
                            continue
                        hd, qt = n // NT, n % NT
                        w = width(qt)
                        if kind == "prep" and mixer == "B":
                            pe.wait_ge(staged, layer * 28 + i * 12 + 3 * (n + 1))
                            turn_blocks([stage_q[:, n % 2, b] for b in range(NT)], BQ)
                            turn_blocks([stage_k[:, n % 2, b] for b in range(NT)], BQ)
                            ready_at[n] = r
                        elif kind == "prep":
                            pe.wait_ge(staged, layer * 28 + i * 2 + (24 + n + 1))
                            turn_blocks([stage_a[:, n % 2, b] for b in range(NT)], P)
                            ready_at[n] = r
                        elif kind == "score":
                            pe.wait_ge(masked, unit + (max(n - 1, 0) + START))
                            if n < 2 and mixer == "B":
                                pe.wait_ge(conv_in, layer * CK + CK)
                            if mixer == "B":
                                pe.wait_ge(turn_out, turn + (ready_at[hd] + START))
                                q, k = qt_buf[0:BQ, hd % 2, qt * P:qt * P + P], kt_buf[0:BQ, hd % 2, 0:w]
                            else:
                                rows = slice(AD * (hd % 2), AD * (hd % 2) + AD)
                                pe.wait_ge(turn_out, turn + (ready_at[hd // 2] + START))
                                q, k = qt_buf[rows, hd // 2, qt * P:qt * P + P], ka_t[rows, 0:w]
                            nc.tensor.matmul(psum[:, n % 2, 0:w], q, k, start=True, stop=True).then_inc(score_ready, 1)
                        elif kind == "turn":
                            pe.wait_ge(prob_ready, unit + (n + 1))
                            turn_blocks([pbuf[:, n % 2, b * P:b * P + P] for b in range(qt + 1)], P)
                            turn_at[n] = r
                        elif kind == "value":
                            pe.wait_ge(turn_out, turn + (turn_at[n] + START))
                            pe.wait_ge(value_out, unit + (max(n - 1, 0) + START))
                            for b in range(qt + 1):
                                if mixer == "B":
                                    v = ukv[:, b, bass.ds(i * (HEADS * P) + (hd * P + BN), BV)]
                                else:
                                    v = h_idx[:, b, G_VA:G_VA + AD]
                                last = nc.tensor.matmul(psum[:, 4 + n % 2, 0:BV], ptbuf[:, n % 2, b * P:b * P + P],
                                                        v, start=(b == 0), stop=(b == qt))
                            last.then_inc(value_ready, 1)
                        elif kind == "out":
                            pe.wait_ge(value_out, unit + (UNITS + START))
                            turn_blocks([ystage[:, b, n * P:n * P + P] for b in range(NT)], P)
                    assert r == per_body

            def down(t, part, first, bank, start, stop):
                arrived(t, first)
                blocks = min(DK, FK - part * DK)
                for b in range(blocks):
                    k, c = part * DK + b, slice(b * P, b * P + P)
                    last = three(psum[:, bank, :], wh[:, t % WS, c], wl[:, t % WS, c], hh[:, k], hl[:, k],
                                 start and b == 0, stop and b == blocks - 1)
                last.then_inc(tile_used, 1)

            def shift(layer, n):
                pe.wait_ge(shift_sum, layer * 2 + (n + 1))
                nc.tensor.matmul(psum[:, 0, :], ones_c[:], sums[n][:, 0], start=True, stop=True).then_inc(shift_ready, 1)

            def norm(layer, n, units):
                def by_token(bank, total, last_block):
                    for b in range(NT):
                        t = slice(b * P, b * P + P)
                        nc.tensor.matmul(psum[:, bank, b:b + 1], total[:, t], ones_d[:, 0:1], start=True, stop=False)
                        last = nc.tensor.matmul(psum[:, bank, b:b + 1], last_block[:, t], ones_d[:, 0:1], start=False,
                                                stop=True)
                    return last

                pe.wait_ge(sum_ready, layer * 2 + (n + 1))
                pe.wait_ge(u_ready, layer * 16 + (8 * (n + 1) + 2))
                by_token(1, sums[n][:, 0], u[:, DK - 1]).then_inc(mean_ready, 1)
                pe.wait_ge(sq_summed, layer * 12 + 6 * (n + 1))
                pe.wait_ge(squared, layer * 16 + 8 * (n + 1))
                by_token(0, sums[n][:, 1], sq[n][:, 1]).then_inc(sq_ready, 1)
                for k in range(2):
                    for unit in units[k:k + 1]:
                        unit()
                    pe.wait_ge(diag_ready, layer * 4 + (2 * n + k + 1))
                    nc.tensor.matmul(psum[:, SPREAD[n] + k, :], ones_1[:], sums[n][:, k], start=True,
                                     stop=True).then_inc(spread, 1)
                for unit in units[2:]:
                    unit()

            def embedding(q, c, layer, first):
                if c == 0:
                    arrived(T_PP + q, first)
                    if q == 0:
                        pe.wait_ge(p_low, layer + 1)
                    if q >= 2:
                        pe.wait_ge(pp_out, layer * DK + 2 * (q - 1))
                h = wh[:, q % WS, 0:4 * P].rearrange("p (k n) -> p k n", k=2)
                lw = wl[:, q % WS, 0:4 * P].rearrange("p (k n) -> p k n", k=2)
                for k in range(2):
                    last = three(psum[:, 4 + 2 * (q % 2) + c, :], h[:, k, c * P:c * P + P], lw[:, k, c * P:c * P + P],
                                 ph[:, k], pl[:, k], k == 0, k == 1)
                if c == 1:
                    last.then_inc(tile_used, 1)

            assert T_PP % WS == 0 and T_FO % WS == 0
            for s in (tile_used, turned, score_ready, value_ready):
                pe.sem_inc(s, START)
            pe.wait_ge(consts_ready, 6)
            pe.sem_inc(passed, 1)
            with pe.Fori(0, L) as layer:
                first = layer * TILES
                for kind, n in FRONT:
                    if kind == "scratch":
                        scratch(n, layer)
                    elif n in tile_group:
                        group(n, layer, first)
                    else:
                        j, value = CONV_PLACE[n]
                        if n == T_CONV:
                            pe.wait_ge(group_out, layer * 40 + 16)
                        if j >= 1:
                            pe.wait_ge(conv_in if value else conv_th, layer * CK + j)
                        if j == 2:
                            pe.wait_ge(group_out, layer * 40 + 36)
                        project(n, first, xh, xl, DK, [(6 if j < 2 else 0) + value])
                pe.wait_ge(group_out, layer * 40 + 40)
                pe.sem_inc(passed, 1)
                attention("B", layer, first)
                attention("A", layer, first)

                pe.wait_ge(conv_done, layer * CK + CK)
                pe.wait_ge(masked, layer * PAIRS + (PAIRS + START))
                for j in range(CK):
                    last = nc.tensor.matmul(psum[:, 0, :], ones_c[:], conv[:, j], start=(j == 0), stop=(j == CK - 1))
                last.then_inc(stat_ready, 1)
                for k in range(DK):
                    if k == 4:
                        for j in range(CK):
                            pe.wait_ge(squared_c, layer * CK + (j + 1))
                            last = nc.tensor.matmul(psum[:, 1, :], ones_c[:], csq[:, j], start=(j == 0),
                                                    stop=(j == CK - 1))
                        last.then_inc(stat_ready, 1)
                    pe.wait_ge(gate_done, layer * 3 * DK + (2 * DK + k - 1 + START))
                    project(T_GC + k, first, xh, xl, DK, [6 + k % 2])
                for q in range(12):
                    pair, br = q // 3, q % 3
                    if q == 0:
                        pe.wait_ge(gate_done, layer * 3 * DK + (3 * DK + START))
                        pe.wait_ge(value_out, layer * PAIRS + (PAIRS + START))
                        pe.wait_ge(y_low, layer * 6 + 2)
                    if q == 2:
                        pe.wait_ge(y_low, layer * 6 + 6)
                    if q >= 2:
                        pe.wait_ge(branch_out, layer * 24 + 2 * (q - 1))
                    project(T_BR + q, first, yh[br], yl[br], 4, [4 + 2 * (q % 2), 5 + 2 * (q % 2)])

                def merged_block(kk):
                    pe.wait_ge(merged_low, layer * DK + (kk + 1))

                for k in range(DK):
                    pe.wait_ge(u_ready, layer * 16 + (k + 1))
                    project(T_OUT + k, first, mh, ml, DK, [2 + k % 2], merged_block if k == 0 else None)
                    if k == 3:
                        shift(layer, 0)
                norm(layer, 0, [lambda q=q, c=c: embedding(q, c, layer, first) for q in range(4) for c in range(2)])
                with pe.Fori(0, 2) as i:
                    for k in range(4):
                        pe.wait_ge(ple_th, layer * DK + i * 4 + (k + 1))

                        def ready(kk):
                            pe.wait_ge(x_ready, layer * 16 + (DK + kk + 1))

                        project(T_PG + k, first + i * 4, xh, xl, DK, [k % 2], ready if k == 0 else None)
                pe.wait_ge(pp_out, layer * DK + DK)
                pe.wait_ge(ple_th, layer * DK + (DK + 2))
                pe.sem_inc(passed, 1)
                with pe.Fori(0, FK // 2) as i:
                    for c in range(2):
                        pe.wait_ge(h_done, layer * (DK + FK) + i * 2 + (DK + c + 1))
                        project(T_FI + 2 * c, first + i * 4, xh, xl, DK, [4 + 2 * c])
                        project(T_FI + 2 * c + 1, first + i * 4, xh, xl, DK, [5 + 2 * c])
                for j in range(DK):
                    pe.wait_ge(u_ready, layer * 16 + (DK + j + 1))
                    for part in range(PARTS):
                        pe.wait_ge(h_done, layer * (DK + FK) + (DK + min(DK * (part + 1), FK) + 2))
                        down(T_FO + PARTS * j + part, part, first, 2 + j % 2, part == 0, part == PARTS - 1)
                    if j == 3:
                        shift(layer, 1)
                norm(layer, 1, [])

        @block.vector
        def _(dve):
            v = nc.vector
            steps = Steps(dve, vec)

            def rope(x, heads, half, c0, dst, done, count):
                x1, x2 = x[:, :, :, 0:half], x[:, :, :, half:2 * half]
                c = cos[:, :, c0:c0 + half].unsqueeze(2).to_broadcast([P, NT, heads, half])
                s = sin[:, :, c0:c0 + half].unsqueeze(2).to_broadcast([P, NT, heads, half])
                n = NT * heads * half
                t1, t2, t3 = [rope_tmp[:, k, 0:n].rearrange("p (t h d) -> p t h d", t=NT, h=heads) for k in range(3)]
                steps.done(v.tensor_tensor(t1, x1, c, ALU.mult))
                steps.done(v.tensor_tensor(t2, x2, s, ALU.mult))
                steps.done(v.tensor_tensor(t3, x1, s, ALU.mult))
                steps.done(v.tensor_tensor(x2, x2, c, ALU.mult))
                steps.wait()
                steps.done(v.tensor_tensor(dst[:, :, :, 0:half], t1, t2, ALU.subtract))
                v.tensor_tensor(dst[:, :, :, half:2 * half], x2, t3, ALU.add).then_inc(done, 1)
                steps.wait()
                dve.wait_ge(done, count)

            dve.sem_inc(u_ready, 2)
            dve.sem_inc(h_done, 2)
            for s in (masked, value_out):
                dve.sem_inc(s, START)
            dve.wait_ge(tables_in, 32)
            ang = rope_tmp[:, 0, 64:256].rearrange("p (t f) -> p t f", t=NT)
            red = rope_tmp[:, 1, 0:192].rearrange("p (t f) -> p t f", t=NT)
            turns = rope_tmp[:, 1, 192:384].rearrange("p (t f) -> p t f", t=NT)
            quarter = rope_tmp[:, 2, 0:192].rearrange("p (t f) -> p t f", t=NT)
            pi = float(np.float32(3.1415925))
            two_pi = [6.28125, float(np.float32(2 * np.pi - 6.28125))]
            two_pi.append(float(2 * np.pi - 6.28125 - two_pi[1]))
            magic = 12582912.0
            two_pi[1] = float(np.float32(round(two_pi[1] * 2 ** 20) / 2 ** 20))
            two_pi[2] = float(2 * np.pi - 6.28125 - two_pi[1])
            steps.stage(0)
            setup = Steps(dve, angle_step)
            setup.done(v.tensor_copy(posf, posi))
            setup.wait()
            for b in range(NT):
                setup.done(v.tensor_scalar(ang[:, b], rope_tmp[:, 0, 0:48], posf[:, b:b + 1], None, ALU.mult))
            setup.wait()
            setup.done(v.tensor_scalar(turns, ang, float(1 / (2 * np.pi)), magic, ALU.mult, ALU.add))
            setup.wait()
            setup.done(v.tensor_scalar(turns, turns, magic, None, ALU.subtract))
            setup.wait()
            src = ang
            for c in two_pi:
                setup.done(v.scalar_tensor_tensor(red, turns, -c, src, ALU.mult, ALU.add))
                setup.wait()
                src = red
            setup.done(v.tensor_scalar(red, red, pi, -pi, ALU.min, ALU.max))
            setup.wait()
            setup.done(v.scalar_tensor_tensor(quarter, red, -1.0, red, ALU.mult, ALU.max))
            setup.wait()
            v.tensor_copy(posf, posf).then_inc(angles, 1)
            v.tensor_scalar(quarter, quarter, -1.0, float(np.pi / 2), ALU.mult, ALU.add).then_inc(angles, 1)
            for j in range(DK):
                dve.wait_ge(x_high, j + 1)
                v.tensor_tensor(xl[:, j], u[:, j], xh[:, j].bitcast(F32), ALU.subtract).then_inc(x_ready, 1)
            dve.wait_ge(tables, 2)
            dve.wait_ge(consts_ready, 6)

            def attention(mixer, layer, base, n_steps):
                steps_, per_body = (STEPS_B, TURNS_B) if mixer == "B" else (STEPS_A, TURNS_A)
                u0, r0, chunk0 = (0, 0, 0) if mixer == "B" else (BH * NT, 2 * TURNS_B, 2)
                scale = BQ ** -0.5 if mixer == "B" else AD ** -0.5
                turn_at, r = {}, 0
                for kind, n in steps_:
                    if kind == "prep":
                        r += 2 if mixer == "B" else 1
                    elif kind in ("turn", "out"):
                        r += 1
                        if kind == "turn":
                            turn_at[n] = r
                with dve.Fori(0, 2) as i:
                    unit = layer * PAIRS + i * UNITS + u0
                    turn = layer * TURNS + i * per_body + r0
                    steps.stage(layer * V_LAYER + i * n_steps + base)

                    def mask(n):
                        qt = n % NT
                        w = width(qt)
                        bias = causal[:, S - w:S] if mixer == "B" or qt == 0 else keep_bias[:, wide(qt):wide(qt) + w]
                        dve.wait_ge(score_ready, unit + (n + 1 + START))
                        dve.wait_ge(turned, turn + ((turn_at[n - 2] if n >= 2 else 0) + START))
                        dve.sem_inc(passed, 1)
                        v.tensor_tensor_reduce(pbuf[:, n % 2, 0:w], psum[:, n % 2, 0:w], bias, -scale, 3e38, ALU.add,
                                               ALU.min, nmax[:, n % 2:n % 2 + 1]).then_inc(masked, 1)

                    def normalise(n):
                        hd, qt = n // NT, n % NT
                        dve.wait_ge(value_ready, unit + (n + 1 + START))
                        if n == 0:
                            dve.wait_ge(turned, turn + START)
                        steps.done(v.reciprocal(rinv[:, n % 2:n % 2 + 1], psums[:, n % 4:n % 4 + 1]))
                        steps.wait()
                        v.tensor_scalar(ystage[:, qt, hd * AD:hd * AD + AD], psum[:, 4 + n % 2, 0:AD],
                                        rinv[:, n % 2:n % 2 + 1], None, ALU.mult).then_inc(value_out, 1)

                    def tap(k):
                        j = i + chunk0
                        h = hconv[:, bass.ds(j, 1), k:k + S].rearrange("p a n -> p (a n)")
                        acc = conv[:, bass.ds(j, 1), :].rearrange("p a n -> p (a n)")
                        w = par[:, bass.ds(i * CW + (PAR["cw"] + chunk0 * CW + k), 1)]
                        if k == 0:
                            b = par[:, bass.ds(i + (PAR["cb"] + chunk0), 1)]
                            steps.done(v.tensor_scalar(acc, h, w, b, ALU.mult, ALU.add))
                        else:
                            steps.wait()
                            ins = v.scalar_tensor_tensor(acc, h, w, acc, ALU.mult, ALU.add)
                            if k < CW - 1:
                                steps.done(ins)
                            else:
                                ins.then_inc(conv_done, 1)

                    for n in range(UNITS):
                        mask(n)
                        if n >= 2:
                            normalise(n - 2)
                        for k in range(2 * n, min(2 * n + 2, CW)):
                            tap(k)
                    normalise(UNITS - 2)
                    normalise(UNITS - 1)
                steps.end("V_ATTN_" + mixer, n_steps)

            def norm(layer, n, start, tile):
                x0, g, b = layer * 16 + 8 * n, ("l1g", "l2g")[n], ("l1b", "l2b")[n]
                total, squares = sums[n][:, 0], sums[n][:, 1]

                def arrive(j):
                    dve.wait_ge(tile_used, first + (tile(j) + 1 + START))
                    v.tensor_tensor(u[:, j], u[:, j], psum[:, 2 + j % 2, :], ALU.add).then_inc(u_ready, 1)

                def add_square(j):
                    dve.wait_ge(squared, x0 + (j + 1))
                    if j > 1:
                        dve.wait_ge(sq_summed, layer * 12 + (6 * n + j - 1))
                    v.tensor_tensor(squares, squares, sq[n][:, j % 2], ALU.add).then_inc(sq_summed, 1)

                start(0)
                start(1)
                steps.wait()
                for j in range(4):
                    arrive(j)
                    start(2 * j + 2)
                    start(2 * j + 3)
                    steps.wait()
                    if j == 1:
                        dve.wait_ge(u_ready, x0 + (2 + 2))
                        v.tensor_tensor(total, u[:, 0], u[:, 1], ALU.add).then_inc(shift_sum, 1)
                dve.wait_ge(shift_ready, layer * 2 + (n + 1))
                dve.wait_ge(u_ready, x0 + (4 + 2))
                for j in range(DK):
                    ins = v.scalar_tensor_tensor(u[:, j], psum[:, 0, :], -2.0, u[:, j], ALU.mult, ALU.add)
                    if j < 4:
                        ins.then_inc(shifted, 1)
                    else:
                        steps.done(ins)
                dve.wait_ge(shifted, layer * 8 + (4 * n + 4))
                steps.done(v.tensor_tensor(total, u[:, 0], u[:, 1], ALU.add))
                steps.wait()
                for j in (2, 3):
                    steps.done(v.tensor_tensor(total, total, u[:, j], ALU.add))
                    steps.wait()
                for j in range(4, DK):
                    arrive(j)
                    if j < DK - 1:
                        dve.wait_ge(u_ready, x0 + (j + 1 + 2))
                        ins = v.tensor_tensor(total, total, u[:, j], ALU.add)
                        if j < DK - 2:
                            steps.done(ins)
                            steps.wait()
                        else:
                            ins.then_inc(sum_ready, 1)
                        for k in {4: (1, 2, 3), 5: (4,), 6: (5, 6)}[j]:
                            add_square(k)

                def diagonal(k, column4):
                    v.tensor_tensor(sums[n][:, k].rearrange("p (t x) -> p t x", t=NT),
                                    ident[:].unsqueeze(1).to_broadcast([P, NT, P]),
                                    column4.unsqueeze(2).to_broadcast([P, NT, P]), ALU.mult).then_inc(diag_ready, 1)

                dve.wait_ge(mean_ready, layer * 2 + (n + 1))
                steps.done(v.tensor_copy(mean4, psum[:, 1, 0:NT]))
                steps.wait()
                steps.done(v.tensor_tensor(scale4, mean4, mean4, ALU.mult))
                steps.wait()
                dve.wait_ge(sq_ready, layer * 2 + (n + 1))
                v.tensor_tensor(var4, psum[:, 0, 0:NT], scale4, ALU.subtract).then_inc(var_ready, 1)
                diagonal(0, mean4)
                dve.wait_ge(sd_ready, layer * 2 + (n + 1))
                steps.done(v.reciprocal(scale4, var4))
                steps.wait()
                diagonal(1, scale4)
                dve.wait_ge(mean_copied, layer * 2 + (n + 1))
                for j in range(CENTERED_DVE):
                    steps.done(v.tensor_tensor(u[:, j], u[:, j], sq[n][:, 0], ALU.subtract))
                steps.wait()
                dve.wait_ge(spread, layer * 4 + (2 * n + 2))
                for j in range(DK + 2):
                    if j < DK:
                        if j >= CENTERED_DVE:
                            dve.wait_ge(centered, layer * 2 * (DK - CENTERED_DVE)
                                        + ((DK - CENTERED_DVE) * n + j - CENTERED_DVE + 1))
                        v.scalar_tensor_tensor(u[:, j], u[:, j], column(g, j), psum[:, SPREAD[n] + 1, :], ALU.mult,
                                               ALU.mult).then_inc(z_ready, 1)
                    if 1 <= j <= DK:
                        dve.wait_ge(x_high, x0 + (DK + j))
                        v.scalar_tensor_tensor(xl[:, j - 1], u[:, j - 1], column(b, j - 1), xh[:, j - 1].bitcast(F32),
                                               ALU.add, ALU.subtract).then_inc(x_ready, 1)
                    if n == 1 and j >= 2:
                        dve.wait_ge(x_ready, x0 + (DK + j - 1))
                        v.tensor_tensor(u[:, j - 2], xh[:, j - 2].bitcast(F32), xl[:, j - 2].bitcast(F32),
                                        ALU.add).then_inc(z_full, 1)

            dve.sem_inc(passed, 1)
            with dve.Fori(0, L) as layer:
                first = layer * TILES
                steps.stage(layer * V_LAYER)
                dve.wait_ge(par_loaded, layer * 16 + 16)
                steps.done(v.tensor_scalar(par[:, 0:HALVED], par[:, 0:HALVED], 0.5, None, ALU.mult))
                dve.wait_ge(group_out, layer * 40 + 4)
                for k in range(2):
                    rope(h_idx[:, :, 192 * k:192 * k + 192].rearrange("p t (h d) -> p t h d", h=3), 3, AD // 2, 0,
                         h_idx[:, :, 192 * k:192 * k + 192].rearrange("p t (h d) -> p t h d", h=3), roped_idx,
                         layer * 2 + (k + 1))
                steps.done(v.tensor_scalar(wi_half, h_idx[:, :, G_WI:G_WI + IH], IH ** -0.5, None, ALU.mult))
                steps.done(v.memset(hconv[:, :, 0:CW - 1], 0.0))
                dve.wait_ge(group_out, layer * 40 + 8)
                rope(h_cq[:, :, QL:QL + BR].unsqueeze(2), 1, BR // 2, AD // 2, key_rope.unsqueeze(2), roped_u,
                     layer * 2 + 1)
                dve.wait_ge(ssq_ready, layer * 8 + (8 + START))
                v.tensor_scalar(rms[:, 0:4], ssq[:, 0:4], 1.0 / QL, RMS_EPS, ALU.mult, ALU.add).then_inc(var_rms, 1)
                v.tensor_scalar(rms[:, 4:8], ssq[:, 4:8], 1.0 / KVL, RMS_EPS, ALU.mult, ALU.add).then_inc(var_rms, 1)
                dve.wait_ge(sd_rms, layer + 1)
                steps.done(v.reciprocal(rms, rms))
                steps.wait()
                for b in range(NT):
                    v.tensor_scalar(h_cq[:, b, 0:QL], h_cq[:, b, 0:QL], rms[:, b:b + 1], None,
                                    ALU.mult).then_inc(normed_c, 1)
                for b in range(NT):
                    v.tensor_scalar(h_ckv[:, b, :], h_ckv[:, b, :], rms[:, 4 + b:5 + b], None,
                                    ALU.mult).then_inc(normed_c, 1)
                dve.wait_ge(group_out, layer * 40 + 16)
                for k in range(2):
                    x = h_qa[:, :, 256 * k:256 * k + 256].rearrange("p t (h d) -> p t h d", h=4)
                    rope(x, 4, AD // 2, 0, x, roped_q, layer * 2 + (k + 1))

                def c_lows(n):
                    dve.wait_ge(scratch_act, layer * SCRATCH + (n + 1))
                    v.scalar_tensor_tensor(cl[:, n - 4], psum[:, n % 4, :], column("gq", n - 4),
                                           ch[:, n - 4].bitcast(F32), ALU.mult, ALU.subtract).then_inc(c_low, 1)

                def conv_input(j):
                    dve.wait_ge(conv_th, layer * CK + (j + 1))
                    dve.wait_ge(tile_used, first + ((T_CONV if j < 2 else T_U + 2) + 2 * j + 2 + START))
                    v.scalar_tensor_tensor(hconv[:, j, CW - 1:CW - 1 + S], th_conv[:, j % 2], 1.0,
                                           psum[:, 7 if j < 2 else 1, :],
                                           ALU.add, ALU.mult).then_inc(conv_in, 1)

                def block_scores(q):
                    for h in range(IH):
                        n = SCRATCH_T + IH * q + h
                        qt = logit(n)[0]
                        w, k = width(qt), IH * q + h
                        sc = scores[:, wide(qt):wide(qt) + w]
                        dve.wait_ge(scratch_act, layer * SCRATCH + (n + 1))
                        if h == 0:
                            v.tensor_scalar(sc, relu[:, k % 2, 0:w], wi_half[:, qt, 0:1], None,
                                            ALU.mult).then_inc(scored, 1)
                        else:
                            dve.wait_ge(scored, layer * 12 + k)
                            v.scalar_tensor_tensor(sc, relu[:, k % 2, 0:w], wi_half[:, qt, h:h + 1], sc, ALU.mult,
                                                   ALU.add).then_inc(scored, 1)
                    dve.wait_ge(scored, layer * 12 + (k + 1))
                    steps.done(v.tensor_tensor(sc[:, w - P:w], sc[:, w - P:w], causal[:, S - P:S], ALU.add))

                for n in range(4, SCRATCH_T):
                    c_lows(n)
                conv_input(0)
                block_scores(0)
                block_scores(1)
                conv_input(1)
                block_scores(2)
                steps.wait()
                for k in range(TOPK // 8):
                    for part in range(2):
                        for qt in range(NT - 1, 0, -1):
                            span = slice(wide(qt), wide(qt) + width(qt))
                            src = scores[:, span] if k == 0 else work[:, span]
                            best = top8[:, 8 * (qt - 1):8 * qt]
                            steps.wait(back=2)
                            dve.sem_inc(passed, 1)
                            if part == 0:
                                steps.done(v.max(best, src))
                            else:
                                steps.done(v.match_replace(work[:, span], best, src, TAKEN))
                    if k == 6:
                        dve.wait_ge(group_out, layer * 40 + 32)
                        x = uq[:].rearrange("p t (h d) -> p t h d", h=BH)[:, :, :, BN:BQ]
                        rope(x, BH, BR // 2, AD // 2, x, roped_u, layer * 2 + 2)
                    if k == 12:
                        conv_input(2)
                steps.wait()
                steps.done(v.tensor_scalar(keep_bias[:], work[:], -2e38, NEG, ALU.is_gt, ALU.mult))
                conv_input(3)
                steps.end("V_FRONT", V_FRONT)
                dve.sem_inc(passed, 1)
                attention("B", layer, VS_B, V_ATTN_B)
                attention("A", layer, VS_A, V_ATTN_A)

                steps.stage(layer * V_LAYER + VS_CONV)
                dve.wait_ge(y_high, layer * 6 + 1)
                v.tensor_tensor(yl[1][:], yb[:], yh[1][:].bitcast(F32), ALU.subtract).then_inc(y_low, 1)
                dve.wait_ge(y_high, layer * 6 + 2)
                v.tensor_tensor(yl[0][:], ya[:], yh[0][:].bitcast(F32), ALU.subtract).then_inc(y_low, 1)
                dve.wait_ge(stat_ready, layer * 2 + 1)
                for j in range(CK):
                    v.tensor_tensor(conv[:, j], conv[:, j], psum[:, 0, :], ALU.subtract).then_inc(centered_c, 1)
                dve.wait_ge(sd_c, layer + 1)
                steps.done(v.reciprocal(rstd_c[:], rstd_c[:]))
                steps.wait()
                for j in range(CK):
                    steps.done(v.tensor_tensor(conv[:, j], conv[:, j], rstd_c[:], ALU.mult))
                    steps.wait()
                    v.tensor_scalar(conv[:, j], conv[:, j], column("clg", j), column("clb", j), ALU.mult,
                                    ALU.add).then_inc(z_conv, 1)
                for j in range(CK + 1):
                    if j < CK:
                        dve.wait_ge(th_ready, layer * CK + (j + 1))
                        v.scalar_tensor_tensor(conv[:, j], th_z[j % 2][:], 1.0, conv[:, j], ALU.add,
                                               ALU.mult).then_inc(y2_ready, 1)
                    if j >= 1:
                        dve.wait_ge(y_high, layer * 6 + (2 + j))
                        v.scalar_tensor_tensor(yl[2][:, j - 1], conv[:, j - 1], 0.5, yh[2][:, j - 1].bitcast(F32),
                                               ALU.mult, ALU.subtract).then_inc(y_low, 1)
                steps.end("V_CONV", V_CONV)

                steps.stage(layer * V_LAYER + VS_BRANCH)
                for q in range(12):
                    pair, br = q // 3, q % 3
                    dve.wait_ge(tile_used, first + (T_BR + q + 1 + START))
                    if q == 0:
                        dve.wait_ge(gate_done, layer * 3 * DK + (3 * DK + START))
                    elif br == 0:
                        dve.wait_ge(merged_low, layer * DK + 2 * pair)
                    for c in range(2):
                        bank, g = psum[:, 4 + 2 * (q % 2) + c, :], (ga, gb, gc)[br][:, 2 * pair + c]
                        if br == 0:
                            v.scalar_tensor_tensor(msum[:, c], g, 1.0, bank, ALU.add, ALU.mult).then_inc(branch_out, 1)
                        else:
                            v.scalar_tensor_tensor(tmp[:], g, 1.0, bank, ALU.add, ALU.mult).then_inc(branch_out, 1)
                            dve.wait_ge(branch_out, layer * 24 + (2 * q + c + 1))
                            ins = v.tensor_tensor(msum[:, c], msum[:, c], tmp[:], ALU.add)
                            if br == 1:
                                steps.done(ins)
                                steps.wait()
                            else:
                                ins.then_inc(merged, 1)
                                dve.wait_ge(merged, layer * DK + (2 * pair + c + 1))
                    if br == 2:
                        for c in range(2):
                            n = 2 * pair + c
                            dve.wait_ge(merged_high, layer * DK + (n + 1))
                            v.scalar_tensor_tensor(ml[:, n], msum[:, c], 0.5, mh[:, n].bitcast(F32), ALU.mult,
                                                   ALU.subtract).then_inc(merged_low, 1)
                steps.end("V_BRANCH", V_BRANCH)
                dve.wait_ge(p_high, layer + 1)
                v.tensor_tensor(pl[:], praw[:], ph[:].bitcast(F32), ALU.subtract).then_inc(p_low, 1)

                steps.stage(layer * V_LAYER + VS_LN1)

                def residual(j):
                    if j < DK:
                        steps.done(v.tensor_scalar(u[:, j], xh[:, j].bitcast(F32), ALPHA, None, ALU.mult))
                        steps.wait()
                        steps.done(v.scalar_tensor_tensor(u[:, j], xl[:, j].bitcast(F32), ALPHA, u[:, j], ALU.mult,
                                                          ALU.add))

                norm(layer, 0, residual, lambda j: T_OUT + j)
                steps.end("V_LN1", V_LN1)

                dve.wait_ge(pp_out, layer * DK + DK)
                dve.sem_inc(passed, 1)
                with dve.Fori(0, 2) as i:
                    steps.stage(layer * V_LAYER + i * V_PG + VS_PG)
                    for k in range(4):
                        j = bass.ds(i * 4 + k, 1)
                        uj, ppj, xhj, xlj = [a[:, j, :].rearrange("p a n -> p (a n)") for a in (u, pp, xh, xl)]
                        dve.wait_ge(ple_th, layer * DK + i * 4 + (k + 1 + 2))
                        steps.done(v.scalar_tensor_tensor(uj, th[:, k % 2, :], 1.0, ppj, ALU.add, ALU.mult))
                        steps.wait()
                        steps.done(v.scalar_tensor_tensor(uj, xhj.bitcast(F32), ALPHA, uj, ALU.mult, ALU.add))
                        steps.wait()
                        v.scalar_tensor_tensor(uj, xlj.bitcast(F32), ALPHA, uj, ALU.mult, ALU.add).then_inc(h_done, 1)
                steps.end("V_PG", V_PG)

                with dve.Fori(0, FK // 2) as i:
                    steps.stage(layer * V_LAYER + i * V_FI + VS_FI)
                    for c in range(2):
                        tc = th[:, c, :]
                        dve.wait_ge(ffn_th, layer * FK + i * 2 + (c + 1))
                        steps.done(v.scalar_tensor_tensor(tc, tc, 1.0, psum[:, 4 + 2 * c, :], ALU.add, ALU.mult))
                        steps.wait()
                        dve.wait_ge(tile_used, first + i * 4 + (T_FI + 2 * c + 2 + START))
                        v.tensor_tensor(tc, tc, psum[:, 5 + 2 * c, :], ALU.mult).then_inc(ffn_s, 1)
                        dve.wait_ge(ffn_high, layer * FK + i * 2 + (c + 1))
                        hhj, hlj = [a[:, bass.ds(i * 2 + c, 1), :].rearrange("p a n -> p (a n)") for a in (hh, hl)]
                        v.scalar_tensor_tensor(hlj, tc, 0.5, hhj.bitcast(F32), ALU.mult,
                                               ALU.subtract).then_inc(h_done, 1)
                steps.end("V_FI", V_FI)
                steps.stage(layer * V_LAYER + VS_LN2)
                norm(layer, 1, lambda j: None, lambda j: T_FO + PARTS * j + PARTS - 1)
                steps.end("V_LN2", V_LN2)


def padded(tiles):
    return np.concatenate([tiles, np.zeros(tiles.shape[:2] + (TILE - tiles.shape[2],), tiles.dtype)], axis=2)


def token_tiles(w, ncol, nk):
    k = w.shape[0] // P
    a = w.reshape(k // nk, nk, P, ncol).transpose(0, 2, 1, 3).reshape(k // nk, P, nk * ncol)
    return padded(a)


def feature_tiles(w, ncol):
    k = w.shape[0] // P
    return w.reshape(k, P, -1, ncol).transpose(2, 1, 0, 3).reshape(-1, P, k * ncol)


def weight_tiles(w_in, w_uq, w_ukv, w_branch, w_out, w_ffn_in, w_ffn_out, w_ple_gate, w_ple_proj):
    def cols(a, b):
        return w_in[:, a:b]

    idx = np.concatenate([cols(C_QI, C_WI), cols(C_KA, C_QI), cols(C_WI, C_CQ)], axis=1)
    cq = np.concatenate([cols(C_CQ, C_CKV), cols(C_KR, C_CA)], axis=1)
    tiles = [token_tiles(idx, 452, 2), token_tiles(cq, 416, 2), token_tiles(cols(C_CKV, C_KR), 256, 4),
             token_tiles(cols(C_QA, C_KA), 512, 2)]
    conv_a, conv_g = feature_tiles(cols(C_CA, C_CG), P), feature_tiles(cols(C_CG, C_GATE), P)
    for j in range(2):
        tiles += [conv_g[j:j + 1], conv_a[j:j + 1]]
    tiles += [token_tiles(w_uq[:, 192 * g:192 * g + 192], 192, 3) for g in range(4)]
    tiles += [token_tiles(w_ukv[:, 512 * g:512 * g + 512], 512, 2) for g in range(2)]
    for j in range(2, CK):
        tiles += [conv_g[j:j + 1], conv_a[j:j + 1]]
    gates = feature_tiles(cols(C_GATE, N_IN), P)
    tiles.append(gates)
    br = [feature_tiles(w_branch[b], 2 * P) for b in range(3)]
    for j in range(4):
        tiles += [br[b][j:j + 1] for b in range(3)]
    tiles.append(feature_tiles(w_out, P))
    tiles.append(padded(feature_tiles(w_ple_proj, 2 * P)))
    tiles.append(feature_tiles(w_ple_gate, P))
    fi = feature_tiles(w_ffn_in, P)
    for j in range(FK):
        tiles += [fi[j:j + 1], fi[FK + j:FK + j + 1]]
    down = w_ffn_out.reshape(FK, P, DK, P).transpose(2, 1, 0, 3)
    for j in range(DK):
        for part in range(PARTS):
            blocks = down[j, :, part * DK:part * DK + DK]
            tiles.append(padded(blocks.reshape(1, P, -1)))
    return np.concatenate(tiles, axis=0)


_OUT = (P, DK, S)


def kernel(x, p, positions, w_in, b_gate, q_norm_g, w_uq, kv_norm_g, w_ukv, conv_w, conv_b, conv_ln_g, conv_ln_b,
           w_branch, w_out, ln1_g, ln1_b, w_ffn_in, w_ffn_out, w_ple_gate, w_ple_proj, ln2_g, ln2_b):
    import concourse.bacc as bacc
    from concourse.bass_utils import run_bass_kernel_spmd

    def arr(a):
        return np.ascontiguousarray(np.asarray(a))

    def columns(a):
        return arr(a).reshape(-1, P).T

    x, p, positions = arr(x), arr(p), arr(positions)
    ws = [arr(a) for a in (w_in, w_uq, w_ukv, w_branch, w_out, w_ffn_in, w_ffn_out, w_ple_gate, w_ple_proj)]
    tiles = np.concatenate([weight_tiles(*[w[i] for w in ws]) for i in range(L)], axis=0)
    tiles = np.concatenate([tiles, tiles[:LEAD]], axis=0)
    params = []
    for i in range(L):
        taps = arr(conv_w)[i].T.reshape(CK, P, CW).transpose(1, 0, 2).reshape(P, CK * CW)
        params.append(np.concatenate(
            [columns(arr(b_gate)[i]), taps, columns(arr(q_norm_g)[i]), columns(arr(kv_norm_g)[i]),
             columns(arr(conv_b)[i]), columns(arr(conv_ln_g)[i]), columns(arr(conv_ln_b)[i]), columns(arr(ln1_g)[i]),
             columns(arr(ln1_b)[i]), columns(arr(ln2_g)[i]), columns(arr(ln2_b)[i])], axis=1))
    freq = [np.float32(1.0) / np.float32(THETA) ** (np.arange(0, n, 2, dtype=np.float32) / np.float32(n))
            for n in (AD, BR)]
    arrays = {
        "in_x": arr(x[0].T.reshape(DK, P, S).transpose(1, 0, 2)),
        "in_ple": arr(p[:, 0].transpose(0, 2, 1).reshape(L, PLE // P, P, S).transpose(0, 2, 1, 3)),
        "in_pos": arr(positions.reshape(NT, P).T),
        "in_freq": arr(np.broadcast_to(np.concatenate(freq).astype(np.float32), (P, 48))),
        "in_weights": arr(tiles),
        "in_params": arr(np.stack(params)),
    }
    nc = bacc.Bacc("TRN2", target_bir_lowering=False, num_devices=1)
    args = [nc.dram_tensor(n, a.shape, mybir.dt.from_np(a.dtype), kind="ExternalInput").ap()
            for n, a in arrays.items()]
    args.append(nc.dram_tensor("out", _OUT, F32, kind="ExternalOutput").ap())
    x_t, ple_t, pos, freq_t, weights, par, out = args
    build(nc, x_t, ple_t, pos, freq_t, weights, par, out)
    got = run_bass_kernel_spmd(nc, [arrays], core_ids=[0]).results[0]["out"]
    return arr(got.transpose(2, 1, 0).reshape(1, S, D))
```
